# Optimizing a Trainium2 kernel written in Bass

```python
import jax, jax.numpy as jnp
from jax import lax
import numpy as np

D_MODEL = 1024
BATCH = 1
SEQ = 1024
DEPTH = 1
DEC_BATCH = 1
DEC_SEQ = 32
PAST_LEN = 128

CHUNK = 64
HEAD_DIM = 64
D_CONV = D_MODEL // 2
CONV_W = 3
SWA_HEADS = 8
SWA_KV = 2
WINDOW = 128
DSA_HEADS = 8
DSA_KV = 2
TOPK_MAX = 256
IDX_HEADS = 4
IDX_DIM = 64
QBLK = 128
D_FF = 2816
FFN_CONV_W = 3
EPS = 1e-6
NEG = -1e30
SCALE = HEAD_DIM ** -0.5
IDX_SCALE = IDX_DIM ** -0.5

SPLIT_SIZES = [D_CONV, D_CONV, D_CONV,
               SWA_HEADS * HEAD_DIM, SWA_KV * HEAD_DIM, SWA_KV * HEAD_DIM,
               DSA_HEADS * HEAD_DIM, DSA_KV * HEAD_DIM, DSA_KV * HEAD_DIM,
               IDX_HEADS * IDX_DIM, IDX_DIM, IDX_HEADS,
               D_MODEL, D_MODEL, D_MODEL]
SPLIT_POINTS = [int(v) for v in np.cumsum(SPLIT_SIZES)[:-1]]
P_IN = int(sum(SPLIT_SIZES))

kernel_name = 'hybrid_streaming_encoder_step'

def rmsnorm(x, g):
    x32 = x.astype(jnp.float32)
    y = x32 * lax.rsqrt(jnp.mean(x32 * x32, axis=-1, keepdims=True) + EPS)
    return y.astype(x.dtype) * g

def causal_dwconv(u, buf, w):
    T = u.shape[1]
    full = jnp.concatenate([buf.astype(u.dtype), u], axis=1)
    y = full[:, 0:T] * w[0]
    for j in range(1, w.shape[0]):
        y = y + full[:, j:j + T] * w[j]
    return y, full[:, T:]

def sink_softmax(s, sink):
    m = jnp.maximum(jnp.max(s, axis=-1, keepdims=True), sink)
    e = jnp.exp(s - m)
    return e / (jnp.sum(e, axis=-1, keepdims=True) + jnp.exp(sink - m))

def swa_prompt(q, k, v, sinks):
    b, T = q.shape[:2]
    nc = T // CHUNK
    nw = WINDOW // CHUNK
    G = SWA_HEADS // SWA_KV
    pad = ((0, 0), (WINDOW, 0), (0, 0), (0, 0))
    kp = jnp.pad(k, pad).reshape(b, nc + nw, CHUNK, SWA_KV, HEAD_DIM)
    vp = jnp.pad(v, pad).reshape(b, nc + nw, CHUNK, SWA_KV, HEAD_DIM)
    kw = jnp.concatenate([kp[:, j:j + nc] for j in range(nw + 1)], axis=2)
    vw = jnp.concatenate([vp[:, j:j + nc] for j in range(nw + 1)], axis=2)
    slot_off = jnp.arange((nw + 1) * CHUNK) // CHUNK - nw
    valid = (jnp.arange(nc)[:, None] + slot_off[None, :]) >= 0
    qc = q.reshape(b, nc, CHUNK, SWA_KV, G, HEAD_DIM)
    s = jnp.einsum('bcqkgd,bcskd->bckgqs', qc, kw).astype(jnp.float32) * SCALE
    s = jnp.where(valid[None, :, None, None, None, :], s, NEG)
    p = sink_softmax(s, sinks.astype(jnp.float32).reshape(1, 1, SWA_KV, G, 1, 1))
    o = jnp.einsum('bckgqs,bcskd->bcqkgd', p.astype(v.dtype), vw)
    return o.reshape(b, T, SWA_HEADS * HEAD_DIM), k[:, T - WINDOW:], v[:, T - WINDOW:]

def swa_step(q, k, v, k_buf, v_buf, sinks):
    b, T = q.shape[:2]
    G = SWA_HEADS // SWA_KV
    kall = jnp.concatenate([k_buf.astype(k.dtype), k], axis=1)
    vall = jnp.concatenate([v_buf.astype(v.dtype), v], axis=1)
    qg = q.reshape(b, T, SWA_KV, G, HEAD_DIM)
    s = jnp.einsum('bqkgd,bskd->bkgqs', qg, kall).astype(jnp.float32) * SCALE
    p = sink_softmax(s, sinks.astype(jnp.float32).reshape(1, SWA_KV, G, 1, 1))
    o = jnp.einsum('bkgqs,bskd->bqkgd', p.astype(v.dtype), vall)
    n = k_buf.shape[1]
    return o.reshape(b, T, SWA_HEADS * HEAD_DIM), kall[:, -n:], vall[:, -n:]

def select_keys(qi, ki, wi, ok, topk):
    logits = jax.nn.relu(jnp.einsum('bqhd,bsd->bqhs', qi, ki).astype(jnp.float32) * IDX_SCALE)
    score = jnp.einsum('bqhs,bqh->bqs', logits, wi.astype(jnp.float32) * (IDX_HEADS ** -0.5))
    if ok is None:
        _, idx = lax.top_k(score, topk)
        valid = jnp.ones(idx.shape, dtype=bool)
    else:
        okb = jnp.broadcast_to(ok, score.shape)
        _, idx = lax.top_k(jnp.where(okb, score, NEG), topk)
        valid = jnp.take_along_axis(okb, idx, axis=-1)
    return idx, valid

def sparse_attend(q, k, v, idx, valid):
    b, Q = q.shape[:2]
    G = DSA_HEADS // DSA_KV
    kg = jax.vmap(lambda kk, ii: kk[ii])(k, idx)
    vg = jax.vmap(lambda vv, ii: vv[ii])(v, idx)
    qg = q.reshape(b, Q, DSA_KV, G, HEAD_DIM)
    s = jnp.einsum('bqkgd,bqskd->bqkgs', qg, kg).astype(jnp.float32) * SCALE
    s = jnp.where(valid[:, :, None, None, :], s, NEG)
    p = jax.nn.softmax(s, axis=-1)
    o = jnp.einsum('bqkgs,bqskd->bqkgd', p.astype(v.dtype), vg)
    return o.reshape(b, Q, DSA_HEADS * HEAD_DIM)

def dsa_prompt(q, k, v, qi, ki, wi):
    b, T = q.shape[:2]
    nblk = T // QBLK
    topk = min(TOPK_MAX, T // 4)
    key_chunk = jnp.arange(T) // CHUNK

    def to_blocks(a):
        return jnp.moveaxis(a.reshape((b, nblk, QBLK) + a.shape[2:]), 1, 0)

    def block(args):
        qb, qib, wib, bi = args
        t = bi * QBLK + jnp.arange(QBLK)
        ok = key_chunk[None, :] <= (t // CHUNK)[:, None]
        idx, valid = select_keys(qib, ki, wib, ok, topk)
        return sparse_attend(qb, k, v, idx, valid)

    o = lax.map(block, (to_blocks(q), to_blocks(qi), to_blocks(wi), jnp.arange(nblk)))
    return jnp.moveaxis(o, 0, 1).reshape(b, T, DSA_HEADS * HEAD_DIM)

def dsa_step(q, k, v, qi, ki, wi, k_past, v_past, ki_past):
    kall = jnp.concatenate([k_past.astype(k.dtype), k], axis=1)
    vall = jnp.concatenate([v_past.astype(v.dtype), v], axis=1)
    kiall = jnp.concatenate([ki_past.astype(ki.dtype), ki], axis=1)
    topk = min(TOPK_MAX, kall.shape[1] // 4)
    idx, valid = select_keys(qi, kiall, wi, None, topk)
    return sparse_attend(q, kall, vall, idx, valid)

def layer(x, is_prompt, conv_a_buf, swa_k_buf, swa_v_buf, dsa_k_past, dsa_v_past, idx_k_past, ffn_buf,
          norm_mix, w_in, conv_a, w_a_out, attn_sinks, w_swa_o, w_dsa_o, w_out,
          norm_ffn, w_gate, w_up, conv_ffn, w_down):
    b, T, _ = x.shape
    h = rmsnorm(x, norm_mix)
    (a_b, a_c, a_x, qb, kb, vb, qc, kc, vc, qi, ki, wi, g_a, g_b, g_c) = jnp.split(h @ w_in, SPLIT_POINTS, axis=-1)
    y_conv, new_conv_a = causal_dwconv(a_c * a_x, conv_a_buf, conv_a)
    br_a = (a_b * y_conv) @ w_a_out
    qb = qb.reshape(b, T, SWA_HEADS, HEAD_DIM)
    kb = kb.reshape(b, T, SWA_KV, HEAD_DIM)
    vb = vb.reshape(b, T, SWA_KV, HEAD_DIM)
    if is_prompt:
        o_b, new_swa_k, new_swa_v = swa_prompt(qb, kb, vb, attn_sinks)
    else:
        o_b, new_swa_k, new_swa_v = swa_step(qb, kb, vb, swa_k_buf, swa_v_buf, attn_sinks)
    br_b = o_b @ w_swa_o
    qc = qc.reshape(b, T, DSA_HEADS, HEAD_DIM)
    kc = kc.reshape(b, T, DSA_KV, HEAD_DIM)
    vc = vc.reshape(b, T, DSA_KV, HEAD_DIM)
    qi = qi.reshape(b, T, IDX_HEADS, IDX_DIM)
    if is_prompt:
        o_c = dsa_prompt(qc, kc, vc, qi, ki, wi)
    else:
        o_c = dsa_step(qc, kc, vc, qi, ki, wi, dsa_k_past, dsa_v_past, idx_k_past)
    br_c = o_c @ w_dsa_o
    merged = jax.nn.sigmoid(g_a) * br_a + jax.nn.sigmoid(g_b) * br_b + jax.nn.sigmoid(g_c) * br_c
    x = x + merged @ w_out
    h2 = rmsnorm(x, norm_ffn)
    g_conv, new_ffn = causal_dwconv(h2 @ w_gate, ffn_buf, conv_ffn)
    x = x + (jax.nn.silu(g_conv) * (h2 @ w_up)) @ w_down
    return x, new_conv_a, new_swa_k, new_swa_v, kc, vc, ki, new_ffn

def setup_inputs(seed: int = 0) -> dict:
    key = jax.random.key(seed)
    ks = jax.random.split(key, 24)

    def nrm(k, shape, scale):
        return jax.random.normal(k, shape, jnp.float32) * scale

    swa_cache = min(WINDOW, PAST_LEN)
    return {
        'x_prompt': nrm(ks[0], (BATCH, SEQ, D_MODEL), 1.0),
        'x_sample': nrm(ks[1], (DEC_BATCH, DEC_SEQ, D_MODEL), 1.0),
        'state_conv_a': nrm(ks[2], (DEPTH, DEC_BATCH, CONV_W - 1, D_CONV), 0.5),
        'cache_swa_k': nrm(ks[3], (DEPTH, DEC_BATCH, swa_cache, SWA_KV, HEAD_DIM), 1.0),
        'cache_swa_v': nrm(ks[4], (DEPTH, DEC_BATCH, swa_cache, SWA_KV, HEAD_DIM), 1.0),
        'cache_dsa_k': nrm(ks[5], (DEPTH, DEC_BATCH, PAST_LEN, DSA_KV, HEAD_DIM), 1.0),
        'cache_dsa_v': nrm(ks[6], (DEPTH, DEC_BATCH, PAST_LEN, DSA_KV, HEAD_DIM), 1.0),
        'cache_idx_k': nrm(ks[7], (DEPTH, DEC_BATCH, PAST_LEN, IDX_DIM), 1.0),
        'state_ffn_conv': nrm(ks[8], (DEPTH, DEC_BATCH, FFN_CONV_W - 1, D_FF), 1.0),
        'norm_mix': 1.0 + nrm(ks[9], (DEPTH, D_MODEL), 0.1),
        'w_in': nrm(ks[10], (DEPTH, D_MODEL, P_IN), D_MODEL ** -0.5),
        'conv_a': nrm(ks[11], (DEPTH, CONV_W, D_CONV), 0.5),
        'w_a_out': nrm(ks[12], (DEPTH, D_CONV, D_MODEL), D_CONV ** -0.5),
        'attn_sinks': nrm(ks[13], (DEPTH, SWA_HEADS), 0.5),
        'w_swa_o': nrm(ks[14], (DEPTH, SWA_HEADS * HEAD_DIM, D_MODEL), (SWA_HEADS * HEAD_DIM) ** -0.5),
        'w_dsa_o': nrm(ks[15], (DEPTH, DSA_HEADS * HEAD_DIM, D_MODEL), (DSA_HEADS * HEAD_DIM) ** -0.5),
        'w_out': nrm(ks[16], (DEPTH, D_MODEL, D_MODEL), D_MODEL ** -0.5),
        'norm_ffn': 1.0 + nrm(ks[17], (DEPTH, D_MODEL), 0.1),
        'w_gate': nrm(ks[18], (DEPTH, D_MODEL, D_FF), D_MODEL ** -0.5),
        'w_up': nrm(ks[19], (DEPTH, D_MODEL, D_FF), D_MODEL ** -0.5),
        'conv_ffn': nrm(ks[20], (DEPTH, FFN_CONV_W, D_FF), 0.5),
        'w_down': nrm(ks[21], (DEPTH, D_FF, D_MODEL), D_FF ** -0.5),
        'norm_final': 1.0 + nrm(ks[22], (D_MODEL,), 0.1),
    }

def reference(x_prompt, x_sample, state_conv_a, cache_swa_k, cache_swa_v, cache_dsa_k, cache_dsa_v,
              cache_idx_k, state_ffn_conv, norm_mix, w_in, conv_a, w_a_out, attn_sinks, w_swa_o,
              w_dsa_o, w_out, norm_ffn, w_gate, w_up, conv_ffn, w_down, norm_final):
    xp, xs = x_prompt, x_sample
    p_ca, p_sk, p_sv, p_dk, p_dv, p_ik, p_fc = [], [], [], [], [], [], []
    s_ca, s_sk, s_sv, s_dk, s_dv, s_ik, s_fc = [], [], [], [], [], [], []
    for i in range(DEPTH):
        lw = (norm_mix[i], w_in[i], conv_a[i], w_a_out[i], attn_sinks[i], w_swa_o[i], w_dsa_o[i],
              w_out[i], norm_ffn[i], w_gate[i], w_up[i], conv_ffn[i], w_down[i])
        zb_a = jnp.zeros((xp.shape[0], CONV_W - 1, D_CONV), xp.dtype)
        zb_f = jnp.zeros((xp.shape[0], FFN_CONV_W - 1, D_FF), xp.dtype)
        xp, ca, sk, sv, dk, dv, ik, fc = layer(xp, True, zb_a, None, None, None, None, None, zb_f, *lw)
        p_ca.append(ca); p_sk.append(sk); p_sv.append(sv); p_dk.append(dk)
        p_dv.append(dv); p_ik.append(ik); p_fc.append(fc)
        xs, ca, sk, sv, dk, dv, ik, fc = layer(xs, False, state_conv_a[i], cache_swa_k[i], cache_swa_v[i],
                                               cache_dsa_k[i], cache_dsa_v[i], cache_idx_k[i],
                                               state_ffn_conv[i], *lw)
        s_ca.append(ca); s_sk.append(sk); s_sv.append(sv); s_dk.append(dk)
        s_dv.append(dv); s_ik.append(ik); s_fc.append(fc)
    y_prompt = rmsnorm(xp, norm_final)
    y_sample = rmsnorm(xs, norm_final)
    return (y_prompt, y_sample,
            jnp.stack(p_ca), jnp.stack(p_sk), jnp.stack(p_sv), jnp.stack(p_dk), jnp.stack(p_dv),
            jnp.stack(p_ik), jnp.stack(p_fc),
            jnp.stack(s_ca), jnp.stack(s_sk), jnp.stack(s_sv), jnp.stack(s_dk), jnp.stack(s_dv),
            jnp.stack(s_ik), jnp.stack(s_fc))


_drawn_inputs = setup_inputs


def setup_inputs(seed=0):
    import zlib

    import numpy as np

    out = dict(_drawn_inputs(seed))
    spreads = {}
    factors = {'attn_sinks': 45.146}
    for name, (base, spread) in spreads.items():
        noise = np.random.default_rng([zlib.crc32(name.encode()), seed]).standard_normal(out[name].shape)
        drawn = base * np.exp(spread * noise) if base else spread * noise
        out[name] = __import__('jax').numpy.asarray(drawn.astype(out[name].dtype))
    for name, factor in factors.items():
        out[name] = (out[name] * factor).astype(out[name].dtype)
    return out
```

```python
from contextlib import ExitStack, contextmanager

import concourse.bass as bass
from concourse import mybir

ALU = mybir.AluOpType
ACT = mybir.ActivationFunctionType
AX = mybir.AxisListType
F32 = mybir.dt.float32
F32R = mybir.dt.float32r

P = 128
D = 1024
KT = D // P
SEQ, DEC = 1024, 32
TOK = SEQ + DEC
BANK = 512
NB = 3
PIECE = TOK // NB
NT = SEQ // P
D_CONV = 512
CT = D_CONV // P
HD = 64
NH, NKV = 8, 2
NJ = NH // NKV
PAST = 128
CHUNK = 64
TOPK, TOPK_S = 256, (PAST + DEC) // 4
IDXH = 4
D_FF = 2816
FT = D_FF // P
FFN_GROUPS = (8, 8, 6)
EPS = 1e-6
NEG = -1e30
TAKEN = -3.0e38
SCALE = HD ** -0.5

C_AB, C_AC, C_AX = 0, 512, 1024
C_QB, C_KB, C_VB = 1536, 2048, 2176
C_QC, C_KC, C_VC = 2304, 2816, 2944
C_QI, C_KI, C_WI = 3072, 3328, 3392
C_G = 3396

J_IDX = 0
J_A = J_IDX + 4
J_GA = J_A + 3 * CT
J_B = J_GA + 2 * KT
J_GB = J_B + NJ + 2
J_C = J_GB + 2 * KT
J_GC = J_C + NJ + 2
J_WO = J_GC + 2 * KT
J_FFN = []
J_DOWN = []
_n = J_WO + KT
for _g in FFN_GROUPS:
    J_FFN.append(_n)
    J_DOWN.append(_n + 2 * _g)
    _n += 2 * _g + KT
J_END = _n

V_NORM, V_CA, V_CF = 0, KT, KT + 3 * CT
VEC_ROWS = V_CF + 3 * FT
S_CA, S_CF = 0, 2 * CT
S_ROWS = S_CF + 2 * FT
N_CA, N_CF = 0, 4 * CT
N_COLS = N_CF + 4 * FT

SEL = [i for i in range(NT) if (i + 1) * P > TOPK]
SEL_AT = {}
_at = 0
for _i in SEL:
    SEL_AT[_i] = _at
    _at += (_i + 1) * P
SEL_COLS = _at


def rows_of(i):
    return P if i < NT else DEC


def apart(eng):
    eng.nop(nofuse=True)


class Steps:

    def __init__(self, eng, sem):
        self.eng, self.sem, self.n, self.marked = eng, sem, 0, 0

    def mark(self, instruction):
        instruction.then_inc(self.sem, 1)
        self.n, self.marked = self.n + 1, self.marked + 1
        return instruction

    def wait(self):
        self.eng.wait_ge(self.sem, self.n)

    @contextmanager
    def loop(self, i, count, per):
        start, marked = self.n, self.marked
        self.n = i * per + start
        yield
        assert self.marked - marked == per, (self.marked - marked, per)
        self.n = start + count * per


def build(nc, ins, outs):
    with ExitStack() as ctx:
        def sem(name):
            return ctx.enter_context(nc.semaphore(name))

        base = (nc.sbuf_base + 63) // 64 * 64
        UNIT = 4 * TOK

        def place(name, shape, dt, units, extra=0):
            return nc.alloc_sbuf_tensor_at(name, shape, dt, offset=base + int(units * UNIT) + extra)

        H_HI = place("h_hi", [P, KT, TOK], F32R, 0)
        X2 = place("residual", [P, KT, TOK], F32, 0)
        H_LO = place("h_lo", [P, KT, TOK], F32R, 8)
        G_HI = place("h2_hi", [P, KT, TOK], F32R, 8)
        Y = place("y", [P, 3, D], F32, 8)
        NF = place("norm_final_rows", [P, D], F32, 8, 3 * 4 * D)
        YJ = place("y_squares", [P, D], F32, 8, 4 * 4 * D)
        MACC = place("merge_sum", [P, KT, TOK], F32, 16)
        M_HI = place("merged_hi", [P, KT, TOK], F32R, 16)
        F_HI = place("ffn_hi", [P, KT, TOK], F32R, 16)
        HN = place("h_rows", [P, 3, D], F32, 16)
        NG = place("norm_mix_rows", [P, D], F32, 16, 3 * 4 * D)
        XJ = place("x_squares", [P, D], F32, 16, 4 * 4 * D)
        XIN = place("x_rows", [P, NT + 1, D], F32, 24)
        XR = place("x_rows_again", [P, NT + 1, D], F32, 24)
        A_HI = place("a_hi", [P, CT, TOK], F32R, 24)
        A_LO = place("a_lo", [P, CT, TOK], F32R, 28)
        QI = place("idx_q", [P, 2, TOK], F32, 24)
        KI = place("idx_k", [P, TOK], F32, 26)
        WIT = place("idx_w", [IDXH, TOK], F32, 27)
        Q_HI = place("q_hi", [P, NJ, TOK], F32R, 24)
        K_HI = place("k_hi", [P, TOK], F32R, 28)
        K_LO = place("k_lo", [P, TOK], F32R, 29)
        Q_LO = place("q_lo", [P, NJ, TOK], F32R, 30)
        O_HI = place("attn_hi", [P, NJ, TOK], F32R, 24)
        O_LO = place("attn_lo", [P, NJ, TOK], F32R, 30)
        G_LO = place("h2_lo", [P, KT, TOK], F32R, 24)
        MASK = place("key_mask", [P, SEL_COLS], F32, 34)
        S_SB = place("idx_scores", [P, 2, D], F32, 38, 4608)
        KI_ROWS = place("idx_k_rows", [P, NT + 1, HD], F32, 38, 4608 + 8192)
        M_LO = place("merged_lo", [P, KT, TOK], F32R, 34)
        F_LO = place("ffn_lo", [P, KT, TOK], F32R, 34)
        V_IN = place("vector_rows", [P, P], F32, 34)
        S_IN = place("state_rows", [P, P], F32, 34, 512)
        T0 = place("t0", [P, TOK + 4], F32, 42)
        T1 = place("t1", [P, TOK + 4], F32, 42, 4256)
        U = place("conv_in", [P, TOK + 4], F32, 42, 2 * 4256)
        T3 = place("t3", [P, TOK + 4], F32, 42, 3 * 4256)
        QS2 = place("sample_idx_q", [P, 2, P], F32, 42, 8704 + 1664)
        WS = place("sample_idx_w", [IDXH, P], F32, 42, 8704 + 2688)
        KSI = place("sample_idx_keys", [P, PAST + DEC], F32, 42, 8704)
        KCI = place("cache_idx_k_rows", [P, P], F32, 42, 8704 + 640)
        V_HI = place("v_hi", [P, NT, P], F32R, 38)
        V_LO = place("v_lo", [P, NT, P], F32R, 38, 4 * NT * P)
        PT_HI = place("probs_t_hi", [P, 2, BANK], F32R, 38, 8192)
        PT_LO = place("probs_t_lo", [P, 2, BANK], F32R, 38, 8192 + 4096)
        PT_S = place("probs_t_sample", [P, 2, BANK], F32, 38, 8192)
        K_T = place("k_columns", [P, TOK], F32, 38)
        V_T = place("v_columns", [P, TOK], F32, 38, 8192)
        PR = place("probs", [P, 4 * D], F32, 38, 16384)
        K_ROWS = place("k_rows", [P, NT + 1, P], F32, 38, 16384 + 2048)
        V_ROWS = place("v_rows", [P, NT + 1, P], F32, 38, 16384 + 2048 + 4608)
        KC = place("cache_k_rows", [P, P], F32, 38, 16384 + 2048 + 9216)
        KS = place("sample_k", [P, PAST + DEC], F32, 38, 32768)
        QS = place("sample_q", [P, P], F32, 38, 32768 + 640)
        wbase = 42 * UNIT + 4 * 4256
        RAW = place("w_raw", [P, 2, KT, P], F32, 0, wbase)
        WHI = place("w_hi", [P, 2, KT, P], F32R, 0, wbase + 8192)
        WLO = place("w_lo", [P, 2, KT, P], F32R, 0, wbase + 16384)
        top = wbase + 24576
        fixed = {}

        def keep(name, cols, rows=P):
            nonlocal top
            fixed[name] = place(name, [rows, cols], F32, 0, top)
            top += (4 * cols + 31) // 32 * 32
            return fixed[name]

        IDENT = keep("ident", P)
        ONES = keep("ones", 1)
        VEC = keep("vectors", VEC_ROWS + S_ROWS)
        NEW = keep("new_states", N_COLS)
        MASK0 = keep("mask_causal", 2 * P)
        MASKW = keep("mask_window", 2 * P)
        MASK_S = keep("mask_sample", PAST + DEC)
        WI = keep("idx_w_rows", IDXH * (NT + 1))
        SINK = keep("sinks", NH)
        SINK_S = keep("sinks_sample", NKV)
        TOP8 = keep("top8", 8)
        NEG_SINK = keep("sinks_negated", NH + NKV)
        STAT = keep("softmax_stats", 3 * 6 * 2)
        VC = keep("cache_v_rows", P)
        VS = keep("sample_v_rows", P)
        SS = keep("norm_stats", 4 * 12)
        assert base + top <= nc.sbuf_usable_end, (base + top, nc.sbuf_usable_end)
        stat = STAT[:, :].rearrange("p (u s h) -> p u s h", u=3, s=6)
        ss = SS[:, :].rearrange("p (s i) -> p s i", s=4)

        def vec(row):
            return VEC[:, row:row + 1]

        def vec_at(i, row):
            return VEC[:, bass.ds(i + row, 1)]

        PS = ctx.enter_context(nc.psum_tensor("ps", [P, 8, BANK], F32))

        raw_full = [sem("raw_full0"), sem("raw_full1")]
        hi_ready, lo_ready = sem("hi_ready"), sem("lo_ready")
        job_done = sem("job_done")
        taken = [sem("taken0"), sem("taken1")]
        x_in = [sem(f"x_in{k}") for k in range(NT + 1)]
        misc_in, x_sq, x_var, x_pow, x_rstd, h_rows, h_t, h_hi, h_lo = (
            sem(n) for n in ("misc_in", "x_sq", "x_var", "x_pow", "x_rstd", "h_rows", "h_t", "h_hi", "h_lo"))
        const_ready, tables_t, tables_ready = sem("const_ready"), sem("tables_t"), sem("tables_ready")
        pool_step, vector_step = sem("pool_step"), sem("vector_step")
        rows_t, rows_out = sem("rows_t"), sem("rows_out")
        side_in = [sem("side_in_idx"), sem("side_in_b"), sem("side_in_c")]
        stored = [sem("stored_idx"), sem("stored_b"), sem("stored_c")]
        staged = sem("staged")
        idx_s, idx_relu, idx_sum = sem("idx_s"), sem("idx_relu"), sem("idx_sum")
        a_sum, a_hi, a_lo = sem("a_sum"), sem("a_hi"), sem("a_lo")
        sum_ready, m_hi, m_lo = sem("sum_ready"), sem("m_hi"), sem("m_lo")
        q_hi = sem("q_hi")
        s_done, masked, negated, exp_done = sem("s_done"), sem("masked"), sem("negated"), sem("exp_done")
        sink_shift, sink_exp, inverse = sem("sink_shift"), sem("sink_exp"), sem("inverse")
        probs = [sem("probs_ready0"), sem("probs_ready1")]
        pt_done, pt_hi, pt_lo, pv_done = sem("pt_done"), sem("pt_hi"), sem("pt_lo"), sem("pv_done")
        v_hi, v_lo = sem("v_hi"), sem("v_lo")
        o_hi, o_lo = sem("o_hi"), sem("o_lo")
        xr_in = [sem(f"xr_in{k}") for k in range(NT // 2 + 1)]
        xr_t, xr_out = sem("xr_t"), sem("xr_out")
        g_hi, g_lo, res_sq, ssq_sum = sem("g_hi"), sem("g_lo"), sem("res_sq"), sem("ssq_sum")
        ss_done, ss_var, ss_pow, ss_rstd, rb_done, rb_ready = (
            sem(n) for n in ("ss_done", "ss_var", "ss_pow", "ss_rstd", "rb_done", "rb_ready"))
        conv_out, silu_done, silu_scaled, f_hi, f_lo = (
            sem(n) for n in ("conv_out", "silu_done", "silu_scaled", "f_hi", "f_lo"))
        y_t, y_sq, y_var, y_pow, y_rstd, y_ready = (
            sem(n) for n in ("y_t", "y_sq", "y_var", "y_pow", "y_rstd", "y_ready"))
        nf_in, ss_clear = sem("nf_in"), sem("ss_clear")
        state_t, state_out = sem("state_t"), sem("state_out")
        y_out = [sem(f"y_out{k}") for k in range(3)]
        states_out = sem("states_out")

        w_in = ins["w_in"][0].rearrange("(k p) n -> p k n", p=P)
        w_a = ins["w_a_out"][0].rearrange("(k p) n -> p k n", p=P)
        w_b = ins["w_swa_o"][0].rearrange("(g j d) n -> g d j n", g=NKV, d=HD)
        w_c = ins["w_dsa_o"][0].rearrange("(g j d) n -> g d j n", g=NKV, d=HD)
        w_o = ins["w_out"][0].rearrange("(k p) n -> p k n", p=P)
        w_g = ins["w_gate"][0].rearrange("(k p) n -> p k n", p=P)
        w_u = ins["w_up"][0].rearrange("(k p) n -> p k n", p=P)
        w_d = ins["w_down"][0].rearrange("(k p) n -> p k n", p=P)

        def x_rows(i):
            return ins["x_prompt"][0, i * P:(i + 1) * P, :] if i < NT else ins["x_sample"][0]

        def group(k, rows=P):
            return PS[0:rows, NB * k:NB * k + NB, 0:PIECE]

        def tokens(ap):
            return ap.rearrange("p (b n) -> p b n", b=NB)

        def tile_at(buf, j):
            return buf[:, bass.ds(j, 1), :].rearrange("p a (b n) -> p (a b) n", b=NB)

        def pairs(kind, first):
            x, q, o = first
            out = []
            for i in [NT] + list(range(NT)):
                sample = i == NT
                window = kind == "window"
                for g in range(1 if sample else NKV):
                    for half in range(1 if sample else 2):
                        if sample:
                            n, first_block, blocks = PAST + DEC, 0, 2
                            mask = None if window else MASK_S[:, :]
                            sinks, negative = SINK_S[:, :], NEG_SINK[:, NH:NH + NKV]
                        else:
                            first_block = max(i - 1, 0) if window else 0
                            blocks = i + 1 - first_block
                            n = blocks * P
                            if window and i > 0:
                                mask = MASKW[:, :]
                            elif n <= TOPK:
                                mask = MASK0[:, 2 * P - n:2 * P]
                            else:
                                mask = MASK[:, SEL_AT[i]:SEL_AT[i] + n]
                            head = g * NJ + 2 * half
                            sinks, negative = SINK[:, head:head + 2], NEG_SINK[:, head:head + 2]
                        size = 1 if sample else 2
                        chunks = [list(range(a, min(a + size, blocks))) for a in range(0, blocks, size)]
                        out.append(dict(x=x, i=i, g=g, half=half, sample=sample, window=window, n=n,
                                        first=first_block, chunks=chunks, q=q, mask=mask, sinks=sinks, negative=negative, ub=x % 3,
                                        o=o, last=sample or half == 1))
                        x += 1
                        q += len(chunks)
                        o += sample or half == 1
            return out, (x, q, o)

        WINDOW, _next = pairs("window", (0, 0, 0))
        SPARSE, _next = pairs("sparse", _next)
        for kind in (WINDOW, SPARSE):
            for r, pair in enumerate(kind):
                if pair["window"]:
                    pair["at"], pair["ahead"] = (0, 12288 // 4, 14336 // 4)[r % 3], 2
                elif pair["sample"] or pair["i"] < 5:
                    pair["at"], pair["ahead"] = 5120 // 4 * (r % 3), 2
                else:
                    pair["at"], pair["ahead"] = 8192 // 4 * ((r + 1) % 2), 1
                former = kind[max(r - (3 if pair["ahead"] == 2 else 2), 0)]
                pair["free"] = former["q"] + len(former["chunks"]) if r >= 3 else 0

        def front(ps, y):
            found = [p for z, p in enumerate(ps) if z - p["ahead"] == y]
            return found[0] if found else None

        def probs_of(pair, h):
            a = pair["at"] + h * pair["n"]
            return PR[:, a:a + pair["n"]]

        def scores_of(pair, h):
            return PS[:, 2 * h:2 * h + 2, :].rearrange("p b n -> p (b n)")[:, 0:pair["n"]]

        def attn_sums(pair, g):
            rows, n = slice(HD * g, HD * (g + 1)), DEC if pair["sample"] else P
            at = pair["i"] * P
            return (PS[rows, 6 + g, 0:NJ * n].rearrange("p (j t) -> p j t", j=NJ),
                    O_HI[rows, :, at:at + n], O_LO[rows, :, at:at + n])

        def groups_of(pair):
            return range(NKV) if pair["sample"] else [pair["g"]]

        R_IDX_C, R_IDX_W, R_IDX_K = 0, 1, 2
        R_B_C, R_B_K, R_B_V = 5, 6, 7
        R_C_C, R_C_K, R_C_V = 10, 11, 14
        TRIPLES = [(0, 4), (4, 8), (8, 9)]
        K_LAST = [(NT - 1, NT + 1)]

        block = ctx.enter_context(nc.Block())

        @block.sync
        def _(sp):
            for i in range(NT + 1):
                sp.dma_start(XIN[0:rows_of(i), i, :], x_rows(i)).then_inc(x_in[i], 16)
                if i == 2:
                    sp.dma_start(RAW[:, 0, 0:4, :], w_in[:, 0:4, C_QI:C_QI + P]).then_inc(raw_full[0], 16)
                    sp.dma_start(RAW[:, 0, 4:8, :], w_in[:, 4:8, C_QI:C_QI + P]).then_inc(raw_full[0], 16)

            def free(n0, i, k):
                sp.wait_ge(lo_ready, n0 + 2 * i + k - 1)
                apart(sp)

            def load(k, dst_src):
                for dst, src in dst_src:
                    sp.dma_start(dst, src).then_inc(raw_full[k], 16)

            def plain(k, src, tiles=KT):
                half = tiles // 2
                return [(RAW[:, k, 0:half, :], src[:, 0:half]), (RAW[:, k, half:tiles, :], src[:, half:tiles])]

            def columns(w, at, width=P):
                return w[:, :, at:at + width]

            load(1, plain(1, columns(w_in, C_QI + P)))
            free(J_IDX, 1, 0)
            load(0, [(RAW[:, 0, :, a * HD:(a + 1) * HD], columns(w_in, C_KI, HD)) for a in range(2)])
            free(J_IDX, 1, 1)
            load(1, [(RAW[:, 1, 0:4, 0:IDXH], w_in[:, 0:4, C_WI:C_WI + IDXH]),
                     (RAW[:, 1, 4:8, 0:IDXH], w_in[:, 4:8, C_WI:C_WI + IDXH])])
            with sp.Fori(0, CT // 2) as i:
                for m in range(6):
                    t, at = m // 3, (C_AB, C_AC, C_AX)[m % 3]
                    free(J_A + 2 * (m // 2), 3 * i, m % 2)
                    load(m % 2, plain(m % 2, w_in[:, :, bass.ds(i * (2 * P) + (at + t * P), P)]))

            def gate_loads(n0, gate, split):
                with sp.Fori(0, KT) as j:
                    free(n0, j, 0)
                    load(0, plain(0, w_in[:, :, bass.ds(j * P + (C_G + gate * D), P)]))
                    free(n0, j, 1)
                    load(1, split(j))

            def head_rows(w):
                return lambda j: [(RAW[HD * g:HD * (g + 1), 1, 0:NJ, :], w[g, :, :, bass.ds(j * P, P)])
                                  for g in range(NKV)]

            def attention_loads(n0, q, kv):
                for k in range(2):
                    free(n0, 0, k)
                    load(k, plain(k, columns(w_in, kv[k])))
                with sp.Fori(0, NJ // 2) as i:
                    for k in range(2):
                        free(n0 + 2, i, k)
                        load(k, [(RAW[:, k, :, g * HD:(g + 1) * HD],
                                  w_in[:, :, bass.ds(i * (2 * HD) + (q + k * HD + g * NJ * HD), HD)])
                                 for g in range(NKV)])

            gate_loads(J_GA, 0, lambda j: plain(1, w_a[:, :, bass.ds(j * P, P)], CT))
            attention_loads(J_B, C_QB, (C_KB, C_VB))
            gate_loads(J_GB, 1, head_rows(w_b))
            attention_loads(J_C, C_QC, (C_KC, C_VC))
            gate_loads(J_GC, 2, head_rows(w_c))
            free(J_WO, 0, 0)
            load(0, plain(0, columns(w_o, 0)))
            sp.wait_ge(job_done, J_WO)
            for i in range(0, NT, 2):
                src = ins["x_prompt"][0, i * P:(i + 2) * P, :].rearrange("(t p) d -> p t d", p=P)
                sp.dma_start(XR[:, i:i + 2, :], src).then_inc(xr_in[i // 2], 16)
            sp.dma_start(XR[0:DEC, NT, :], x_rows(NT)).then_inc(xr_in[NT // 2], 16)
            free(J_WO, 0, 1)
            load(1, plain(1, columns(w_o, P)))
            with sp.Fori(1, KT // 2) as i:
                for k in range(2):
                    free(J_WO, i, k)
                    load(k, plain(k, w_o[:, :, bass.ds(i * (2 * P) + k * P, P)]))
            f0 = 0
            for g, nf in enumerate(FFN_GROUPS):
                with sp.Fori(0, nf) as f:
                    free(J_FFN[g], f, 0)
                    load(0, plain(0, w_g[:, :, bass.ds(f * P + f0 * P, P)]))
                    free(J_FFN[g], f, 1)
                    load(1, plain(1, w_u[:, :, bass.ds(f * P + f0 * P, P)]))
                with sp.Fori(0, KT // 2) as i:
                    for k in range(2):
                        free(J_DOWN[g], i, k)
                        load(k, plain(k, w_d[:, f0:f0 + nf, bass.ds(i * (2 * P) + k * P, P)], nf))
                f0 += nf
            sp.wait_ge(job_done, J_DOWN[-1])
            sp.dma_start(NF[:, :], ins["norm_final"].rearrange("(a n) -> a n", a=1).broadcast_to([P, D])).then_inc(nf_in, 16)
            for i in range(NT + 1):
                sp.wait_ge(y_ready, i + 1)
                out = outs[0][0, i * P:(i + 1) * P, :] if i < NT else outs[1][0]
                sp.dma_start(out, Y[0:rows_of(i), i % 3, :]).then_inc(y_out[i % 3], 16)
            for k in range(3):
                sp.wait_ge(y_out[k], 16 * len(range(k, NT + 1, 3)))

        @block.gpsimd
        def _(pool):
            step = Steps(pool, pool_step)

            def load(dst, src, s):
                pool.dma_start(dst, src).then_inc(s, 16)

            load(NG[:, :], ins["norm_mix"].broadcast_to([P, D]), misc_in)
            tile_rows = lambda a: a.rearrange("r (t p) -> (r t) p", p=P)
            load(V_IN[V_NORM:V_NORM + KT, :], tile_rows(ins["norm_ffn"]), misc_in)
            load(V_IN[V_CA:V_CA + 3 * CT, :], tile_rows(ins["conv_a"][0]), misc_in)
            load(V_IN[V_CF:V_CF + 3 * FT, :], tile_rows(ins["conv_ffn"][0]), misc_in)
            load(S_IN[S_CA:S_CA + 2 * CT, :], tile_rows(ins["state_conv_a"][0, 0]), misc_in)
            load(S_IN[S_CF:S_CF + 2 * FT, :], tile_rows(ins["state_ffn_conv"][0, 0]), misc_in)
            load(SINK[:, :], ins["attn_sinks"].broadcast_to([P, NH]), misc_in)
            step.mark(nc.gpsimd.memset(IDENT[:, :], 0.0))
            step.wait()
            nc.gpsimd.affine_select(out=IDENT[:, :], in_=IDENT[:, :], compare_op=ALU.not_equal, fill=1.0,
                                    base=0, pattern=[[-1, P]], channel_multiplier=1).then_inc(const_ready, 1)
            nc.gpsimd.memset(ONES[:, :], 1.0).then_inc(const_ready, 1)
            for a in range(2):
                load(KCI[:, a * HD:(a + 1) * HD], ins["cache_idx_k"][0, 0], side_in[0])

            def power(src, dst, ready, done, n):
                pool.wait_ge(ready, n)
                nc.gpsimd.tensor_tensor(dst, src[0], src[1], ALU.pow).then_inc(done, 1)

            def half(rows):
                return ss[0:rows, 3, 0:1]

            for m in range((NT + 1) // 3):
                power((ss[:, 1, 3 * m:3 * m + 3], half(P).broadcast_to([P, 3])), ss[:, 2, 3 * m:3 * m + 3],
                      x_var, x_pow, m + 1)

            pool.wait_ge(rows_out, R_IDX_K + 3)
            out = outs[7][0, 0].rearrange("(t p) d -> p t d", p=P)
            pool.dma_start(out, KI_ROWS[:, 0:NT, :]).then_inc(stored[0], 16)
            pool.dma_start(outs[14][0, 0], KI_ROWS[0:DEC, NT, :]).then_inc(stored[0], 16)

            def kv(d):
                return d.rearrange("t g d -> t (g d)")

            pool.wait_ge(job_done, J_B)
            pool.wait_ge(a_lo, CT + 1)
            load(KC[:, :], kv(ins["cache_swa_k"][0, 0]), side_in[1])
            load(VC[:, :], kv(ins["cache_swa_v"][0, 0]), side_in[1])
            pool.wait_ge(side_in[1], 32)
            for src, o_s in ((KC, 10), (VC, 11)):
                pool.dma_start(kv(outs[o_s][0, 0])[0:P - DEC, :], src[DEC:P, :]).then_inc(stored[1], 16)
            pool.wait_ge(rows_out, R_B_V + 3)
            for new, o_p, o_s in ((K_ROWS, 3, 10), (V_ROWS, 4, 11)):
                pool.dma_start(kv(outs[o_p][0, 0]), new[:, NT - 1, :]).then_inc(stored[1], 16)
                pool.dma_start(kv(outs[o_s][0, 0])[P - DEC:P, :], new[0:DEC, NT, :]).then_inc(stored[1], 16)

            pool.wait_ge(job_done, J_GB + 2)
            pool.wait_ge(stored[1], 16 * 6)
            load(KC[:, :], kv(ins["cache_dsa_k"][0, 0]), side_in[2])
            load(VC[:, :], kv(ins["cache_dsa_v"][0, 0]), side_in[2])
            pool.wait_ge(rows_out, R_C_V + 3)
            for new, o_p, o_s in ((K_ROWS, 5, 12), (V_ROWS, 6, 13)):
                out = kv(outs[o_p][0, 0]).rearrange("(t p) d -> p t d", p=P)
                pool.dma_start(out, new[:, 0:NT, :]).then_inc(stored[2], 16)
                pool.dma_start(kv(outs[o_s][0, 0]), new[0:DEC, NT, :]).then_inc(stored[2], 16)

            pool.wait_ge(ss_var, 1)
            nc.gpsimd.tensor_tensor(ss[0:96, 2, 0:11], ss[0:96, 1, 0:11],
                                    ss[0:96, 3, 0:1].broadcast_to([96, 11]), ALU.pow).then_inc(ss_pow, 1)
            pool.wait_ge(rb_ready, 3)
            at = 0
            for g, nf in enumerate(FFN_GROUPS):
                with pool.Fori(0, nf) as f:
                    pool.wait_ge(silu_done, f + (at + 1))
                    nc.gpsimd.tensor_tensor(T0[:, 0:TOK], T0[:, 0:TOK], T3[:, 0:TOK],
                                            ALU.mult).then_inc(silu_scaled, 1)
                at += nf
            for i in range(NT + 1):
                r = rows_of(i)
                power((ss[0:r, 1, i:i + 1], half(r)), ss[0:r, 2, i:i + 1], y_var, y_pow, i + 1)
            pool.wait_ge(state_out, 1)
            rows = U[0:N_COLS, 0:P]
            for at, width, o_p, o_s in ((N_CA, CT, 2, 9), (N_CF, FT, 8, 15)):
                for s, o in ((0, o_p), (1, o_s)):
                    a = at + 2 * s * width
                    pool.dma_start(tile_rows(outs[o][0, 0]), rows[a:a + 2 * width, :]).then_inc(states_out, 16)
            pool.wait_ge(stored[0], 32)
            pool.wait_ge(stored[1], 16 * 6)
            pool.wait_ge(stored[2], 16 * 4)
            pool.wait_ge(states_out, 16 * 4)

        @block.tensor
        def _(pe):
            def project(n0, i, k, hi, lo, tiles=KT, rows=P, ready=None, between=None):
                pe.wait_ge(lo_ready, n0 + 2 * i + k + 1)
                if not (isinstance(i, int) and n0 + 2 * i == 0):
                    pe.wait_ge(taken[k], n0 // 2 + i)
                for t in range(tiles):
                    if ready:
                        pe.wait_ge(ready[0], ready[1] + t + 1)
                    for w, x in ((WHI, hi), (WHI, lo), (WLO, hi)):
                        for b in range(NB):
                            last = nc.tensor.matmul(
                                PS[0:rows, NB * k + b, 0:PIECE], w[:, k, t, 0:rows],
                                x[:, t, b * PIECE:(b + 1) * PIECE],
                                start=t == 0 and w is WHI and x is hi,
                                stop=t == tiles - 1 and w is WLO)
                    if t == tiles - 1:
                        last.then_inc(job_done, 1)
                    if between and t in between:
                        between[t]()

            def transpose(out, in_, s=None):
                r = in_.shape[0]
                p0 = in_.start_partition()
                last = nc.tensor.transpose(out, in_, IDENT[p0:p0 + r, p0:p0 + r])
                if s is not None:
                    last.then_inc(s, 1)

            pe.wait_ge(const_ready, 2)
            pe.wait_ge(misc_in, 16 * 7)
            transpose(PS[:, 6, 0:VEC_ROWS], V_IN[0:VEC_ROWS, :])
            transpose(PS[:, 6, P:P + S_ROWS], S_IN[0:S_ROWS, :], tables_t)
            for i in range(NT + 1):
                r = rows_of(i)
                pe.wait_ge(h_rows, i + 1)
                if i >= 3:
                    pe.wait_ge(h_lo, i - 2)
                for j in range(KT):
                    transpose(PS[:, 2 * (i % 3) + j // 4, (j % 4) * P:(j % 4) * P + r],
                              HN[0:r, i % 3, j * P:(j + 1) * P], h_t if j == KT - 1 else None)
            pe.wait_ge(h_lo, NT + 1)

            for i in range(2):
                for k in range(2):
                    rows = IDXH if (i, k) == (1, 1) else P
                    project(J_IDX, i, k, H_HI, H_LO, rows=rows)
            pe.wait_ge(side_in[0], 32)
            pe.wait_ge(tables_ready, 1)
            transpose(PS[:, 6, 0:P], KCI[:, :], rows_t)
            pe.wait_ge(taken[1], 2)
            pe.wait_ge(staged, 1)
            for i in SEL:
                transpose(PS[:, 7, IDXH * i:IDXH * (i + 1)], WIT[:, i * P:(i + 1) * P])
            transpose(PS[:, 7, IDXH * NT:IDXH * (NT + 1)], WS[:, :], rows_t)
            pe.wait_ge(taken[0], 2)
            for m, (a, b) in enumerate(TRIPLES):
                pe.wait_ge(rows_out, R_IDX_K + m - 1)
                for i in range(a, b):
                    r = rows_of(i)
                    transpose(PS[0:r, 6 + m % 2, (i - a) * HD:(i - a + 1) * HD],
                              KI[0:HD, i * P:i * P + r], rows_t if i == b - 1 else None)
            c = 0
            pe.wait_ge(taken[1], 2)
            for i in SEL + [NT]:
                n = (i + 1) * P if i < NT else PAST + DEC
                if i == NT:
                    pe.wait_ge(staged, 3)
                for h in range(IDXH):
                    p0 = HD * (h % 2)
                    if c >= 2:
                        pe.wait_ge(idx_relu, c - 1)
                    keys = KI if i < NT else KSI
                    q = QI[p0:p0 + HD, h // 2, i * P:(i + 1) * P] if i < NT else QS2[p0:p0 + HD, h // 2, :]
                    for a in range(0, n, BANK):
                        b = min(a + BANK, n)
                        last = nc.tensor.matmul(PS[:, 2 * (c % 2) + a // BANK, 0:b - a], q,
                                                keys[p0:p0 + HD, a:b], start=True, stop=True)
                    last.then_inc(idx_s, 1)
                    c += 1
            pe.wait_ge(idx_relu, c)

            with pe.Fori(0, CT // 2) as i:
                for m in range(6):
                    project(J_A + 2 * (m // 2), 3 * i, m % 2, H_HI, H_LO)
            def gates(n0, hi, lo, ready, count):
                with pe.Fori(0, KT) as j:
                    project(n0, j, 0, H_HI, H_LO)
                    pe.wait_ge(ready, count)
                    project(n0, j, 1, hi, lo, tiles=CT)

            gates(J_GA, A_HI, A_LO, a_lo, CT + 1)

            def row_group(r, src, a, b):
                pe.wait_ge(rows_out, r - 1)
                for i in range(a, b):
                    n = rows_of(i)
                    transpose(PS[0:n, 6 + r % 2, (i - a) * P:(i - a + 1) * P],
                              src[:, i * P:i * P + n], rows_t if i == b - 1 else None)

            def attention_jobs(n0, side, r_c, k_tiles):
                def cached():
                    pe.wait_ge(side_in[side], 32)
                    pe.wait_ge(rows_out, r_c)
                    transpose(PS[:, 6 + r_c % 2, 0:P], KC[:, :], rows_t)

                def group_of(r, src, a, b):
                    return lambda: row_group(r, src, a, b)

                for k in range(2):
                    project(n0, 0, k, H_HI, H_LO)
                pe.wait_ge(taken[0], n0 // 2 + 1)
                keys = [group_of(r_c + 1 + m, K_T, a, b) for m, (a, b) in enumerate(k_tiles)]
                r_v = r_c + 1 + len(keys)
                project(n0, 1, 0, H_HI, H_LO, between={1: cached, **{3 + 2 * m: g for m, g in enumerate(keys)}})
                pe.wait_ge(taken[1], n0 // 2 + 1)
                project(n0, 1, 1, H_HI, H_LO)
                values = [group_of(r_v + m, V_T, a, b) for m, (a, b) in enumerate(TRIPLES)]
                project(n0, 2, 0, H_HI, H_LO, between=dict(zip((0, 1, 5), values)))
                project(n0, 2, 1, H_HI, H_LO)
                for k in range(2):
                    pe.wait_ge(taken[k], n0 // 2 + 3)
                pe.wait_ge(rows_out, r_v + 3)

            def qk(pair, h):
                x, n = pair["x"], pair["n"]
                if x > 0:
                    pe.wait_ge(masked, 2 * (x - 1) + h + 1)
                if pair["sample"]:
                    pe.wait_ge(staged, 5 if pair["window"] else 7)
                    rows = slice(HD * h, HD * (h + 1))
                    last = nc.tensor.matmul(PS[:, 2 * h, 0:n], QS[rows, :], KS[rows, :], start=True, stop=True)
                else:
                    rows = slice(HD * pair["g"], HD * (pair["g"] + 1))
                    j, at = 2 * pair["half"] + h, pair["i"] * P
                    for a in range(0, n, BANK):
                        b = min(a + BANK, n)
                        k0 = pair["first"] * P
                        for q, k in ((Q_HI, K_HI), (Q_HI, K_LO), (Q_LO, K_HI)):
                            last = nc.tensor.matmul(PS[:, 2 * h + a // BANK, 0:b - a], q[rows, j, at:at + P],
                                                    k[rows, k0 + a:k0 + b], start=q is Q_HI and k is K_HI,
                                                    stop=q is Q_LO)
                last.then_inc(s_done, 1)

            def pt(pair, c):
                q = pair["q"] + c
                for h in range(2):
                    pe.wait_ge(probs[h], pair["x"] + 1)
                if q >= 2:
                    pe.wait_ge(pt_hi, q - 1)
                    pe.wait_ge(pt_lo, q - 1)
                for at, b in enumerate(pair["chunks"][c]):
                    rows = DEC if pair["sample"] and b == 1 else P
                    for h in range(2):
                        last = h == 1 and b == pair["chunks"][c][-1]
                        transpose(PS[0:rows, 4 + q % 2, (2 * at + h) * P:(2 * at + h + 1) * P],
                                  probs_of(pair, h)[:, b * P:b * P + rows], pt_done if last else None)

            def pv(pair, c):
                q, g = pair["q"] + c, pair["g"]
                pe.wait_ge(pt_hi, q + 1)
                pe.wait_ge(pt_lo, q + 1)
                if c == 0 and pair["half"] == 0:
                    before = pair["o"] - (1 if pair["sample"] or (pair["i"], g) == (0, 0) else 2)
                    if before >= 0:
                        pe.wait_ge(o_lo, before + 1)
                blocks = len(pair["chunks"]) * (1 if pair["sample"] else 2)
                for at, b in enumerate(pair["chunks"][c]):
                    if pair["sample"]:
                        v, rows = (VC[:, :], P) if b == 0 else (VS[0:DEC, :], DEC)
                        for h in range(NKV):
                            last = nc.tensor.matmul(PS[:, 6 + h, 0:P], v, PT_S[0:rows, q % 2, h * P:(h + 1) * P],
                                                    start=b == 0, stop=b == 1)
                        continue
                    key = pair["first"] + b
                    end = b == pair["chunks"][-1][-1]
                    for v, p in ((V_HI, PT_HI), (V_HI, PT_LO), (V_LO, PT_HI)):
                        last = nc.tensor.matmul(PS[:, 6 + g, 2 * P * pair["half"]:2 * P * (pair["half"] + 1)],
                                                v[:, key, :], p[:, q % 2, 2 * P * at:2 * P * (at + 1)],
                                                start=b == 0 and v is V_HI and p is PT_HI,
                                                stop=end and v is V_LO)
                last.then_inc(pv_done, 1)

            def attend(ps):
                for pair in ps[0:2]:
                    qk(pair, 0)
                    qk(pair, 1)
                for y, pair in enumerate(ps):
                    ahead = front(ps, y)
                    if ahead:
                        qk(ahead, 0)
                        qk(ahead, 1)
                    pt(pair, 0)
                    if y > 0:
                        pv(ps[y - 1], len(ps[y - 1]["chunks"]) - 1)
                    for c in range(1, len(pair["chunks"])):
                        pt(pair, c)
                        pv(pair, c - 1)
                last = ps[-1]
                pv(last, len(last["chunks"]) - 1)
                pe.wait_ge(masked, 2 * (last["x"] + 1))

            attention_jobs(J_B, 1, R_B_C, K_LAST)
            attend(WINDOW)
            gates(J_GB, O_HI, O_LO, o_lo, WINDOW[-1]["o"] + 1)
            attention_jobs(J_C, 2, R_C_C, TRIPLES)
            attend(SPARSE)
            gates(J_GC, O_HI, O_LO, o_lo, SPARSE[-1]["o"] + 1)

            def x_tile(i):
                def run():
                    pe.wait_ge(xr_in[i // 2], 16)
                    pe.wait_ge(xr_out, i)
                    r = rows_of(i)
                    for j in range(KT):
                        transpose(PS[:, 6 + j // 4, (j % 4) * P:(j % 4) * P + r],
                                  XR[0:r, i, j * P:(j + 1) * P], xr_t if j == KT - 1 else None)
                return run

            project(J_WO, 0, 0, M_HI, M_LO, ready=(m_lo, 0), between={t: x_tile(t - 5) for t in (5, 6, 7)})
            project(J_WO, 0, 1, M_HI, M_LO, between={t: x_tile(t + 3) for t in range(6)})
            with pe.Fori(1, KT // 2) as i:
                for k in range(2):
                    project(J_WO, i, k, M_HI, M_LO)

            for g, nf in enumerate(FFN_GROUPS):
                first = 0
                if g == 0:
                    first = 1
                    project(J_FFN[0], 0, 0, G_HI, G_LO, ready=(g_lo, 0))
                    pe.wait_ge(ssq_sum, KT + 1)
                    for i in range(11):
                        last = nc.tensor.matmul(PS[0:96, 6, i:i + 1], T0[:, i * 96:(i + 1) * 96],
                                                ONES[:, :], start=True, stop=True)
                    last.then_inc(ss_done, 1)
                    project(J_FFN[0], 0, 1, G_HI, G_LO)
                    pe.wait_ge(ss_rstd, 1)
                    for m in range(3):
                        if m == 2:
                            pe.wait_ge(rb_ready, 1)
                        tiles = range(5 * m, min(5 * m + 5, 11))
                        for i in tiles:
                            last = nc.tensor.matmul(PS[:, 7 - m % 2, (i - 5 * m) * 96:(i - 5 * m + 1) * 96],
                                                    ss[0:96, 2, i:i + 1].broadcast_to([96, P]),
                                                    IDENT[0:96, 0:96], start=True, stop=True)
                        last.then_inc(rb_done, 1)
                with pe.Fori(first, nf) as f:
                    project(J_FFN[g], f, 0, G_HI, G_LO)
                    project(J_FFN[g], f, 1, G_HI, G_LO)
                with pe.Fori(0, KT // 2) as i:
                    for k in range(2):
                        project(J_DOWN[g], i, k, F_HI, F_LO, tiles=nf, ready=(f_lo, sum(FFN_GROUPS[:g])))
            pe.wait_ge(rb_ready, 3)
            transpose(PS[0:N_COLS, 6, 0:P], NEW[:, :], state_t)
            for k in range(2):
                pe.wait_ge(taken[k], J_END // 2)
            for i in range(NT + 1):
                r = rows_of(i)
                if i >= 3:
                    pe.wait_ge(y_ready, i - 2)
                for j in range(KT):
                    transpose(PS[0:r, 2 * (i % 3) + j // 4, (j % 4) * P:(j % 4 + 1) * P],
                              X2[:, j, i * P:i * P + r], y_t if j == KT - 1 else None)

        @block.scalar
        def _(act):
            def copy(out, in_):
                return nc.scalar.activation(out, in_, ACT.Copy)

            def split(n0, i, k):
                act.wait_ge(raw_full[k], 32 * (n0 // 2 + i + 1))
                if not (isinstance(i, int) and n0 + 2 * i == 0):
                    act.wait_ge(job_done, n0 + 2 * i + k - 1)
                copy(WHI[:, k, :, :], RAW[:, k, :, :]).then_inc(hi_ready, 1)

            def following(n0, i, k):
                split(n0, i, 1) if k == 0 else split(n0, i + 1, 0)

            def done(n0, i, k):
                act.wait_ge(job_done, n0 + 2 * i + k + 1)

            def h_high(i):
                r = rows_of(i)
                act.wait_ge(h_t, i + 1)
                src = PS[:, 2 * (i % 3):2 * (i % 3) + 2, :].rearrange("p b (j t) -> p (b j) t", t=P)
                copy(H_HI[:, :, i * P:i * P + r], src[:, :, 0:r]).then_inc(h_hi, 1)

            for i in range(NT + 1):
                r = rows_of(i)
                if i == 5:
                    act.wait_ge(tables_t, 1)
                    copy(VEC[:, 0:VEC_ROWS], PS[:, 6, 0:VEC_ROWS])
                    copy(VEC[:, VEC_ROWS:VEC_ROWS + S_ROWS], PS[:, 6, P:P + S_ROWS]).then_inc(tables_ready, 1)
                act.wait_ge(x_in[i], 16)
                if i >= 1:
                    act.wait_ge(x_sq, i)
                else:
                    act.wait_ge(ss_clear, 1)
                nc.scalar.activation(XJ[0:r, :], XIN[0:r, i, :], ACT.Square,
                                     accum_out=ss[0:r, 0, i:i + 1]).then_inc(x_sq, 1)
                if i >= 5:
                    h_high(i - 5)
            for i in range(NT - 4, NT + 1):
                h_high(i)

            split(0, 0, 0)
            for n in range(4):
                i, k = n // 2, n % 2
                following(J_IDX, i, k)
                done(J_IDX, i, k)
                if n < 2:
                    nc.scalar.mul(tokens(QI[:, n, :]), group(k), SCALE).then_inc(taken[k], 1)
                elif n == 2:
                    copy(tokens(KI[:, :]), group(k)).then_inc(taken[k], 1)
                else:
                    nc.scalar.mul(tokens(WIT[:, :]), group(k, IDXH), IDXH ** -0.5).then_inc(taken[k], 1)
            act.wait_ge(rows_t, R_IDX_C + 1)
            act.wait_ge(tables_ready, 1)
            copy(KSI[:, 0:PAST], PS[:, 6, 0:PAST]).then_inc(rows_out, 1)
            act.wait_ge(rows_t, R_IDX_W + 1)
            w0 = IDXH * SEL[0]
            copy(WI[:, w0:IDXH * (NT + 1)], PS[:, 7, w0:IDXH * (NT + 1)]).then_inc(rows_out, 1)
            for m, (a, b) in enumerate(TRIPLES):
                act.wait_ge(rows_t, R_IDX_K + m + 1)
                r = rows_of(a)
                copy(KI_ROWS[0:r, a:b, :], PS[0:r, 6 + m % 2, 0:(b - a) * HD].rearrange("p (t d) -> p t d", d=HD)
                     ).then_inc(rows_out, 1)
            c = 0
            for i in SEL + [NT]:
                n = (i + 1) * P if i < NT else PAST + DEC
                for h in range(IDXH):
                    act.wait_ge(idx_s, c + 1)
                    if c >= 2:
                        act.wait_ge(idx_sum, c - 1)
                    src = PS[:, 2 * (c % 2):2 * (c % 2) + 2, :].rearrange("p b n -> p (b n)")[:, 0:n]
                    nc.scalar.activation(S_SB[:, c % 2, 0:n], src, ACT.Relu).then_inc(idx_relu, 1)
                    c += 1

            with act.Fori(0, CT // 2) as i:
                for m in range(6):
                    n0, k, t = J_A + 2 * (m // 2), m % 2, m // 3
                    following(n0, 3 * i, k)
                    done(n0, 3 * i, k)
                    if m % 3 == 0:
                        act.wait_ge(a_lo, 2 * i + t + 1)
                        copy(tokens(T0[:, 0:TOK]), group(k)).then_inc(taken[k], 1)
                    elif m % 3 == 1:
                        copy(tokens(T1[:, 0:TOK]), group(k)).then_inc(taken[k], 1)
                    else:
                        act.wait_ge(a_sum, 2 * i + t + 1)
                        apart(act)
                        copy(tile_at(A_HI, 2 * i + t), tokens(T1[:, 0:TOK])).then_inc(a_hi, 1)

            def gates(n0, merged=False):
                with act.Fori(0, KT) as j:
                    following(n0, j, 0)
                    done(n0, j, 0)
                    act.wait_ge(taken[1], n0 // 2 + j)
                    nc.scalar.activation(tokens(T0[:, 0:TOK]), group(0), ACT.Sigmoid).then_inc(taken[0], 1)
                    following(n0, j, 1)
                    if merged:
                        act.wait_ge(sum_ready, j + 1)
                        apart(act)
                        copy(tile_at(M_HI, j), tokens(T3[:, 0:TOK])).then_inc(m_hi, 1)

            gates(J_GA)

            def attention_jobs(n0, side, r_c, k_tiles):
                following(n0, 0, 0)
                done(n0, 0, 0)
                if n0 == J_B:
                    act.wait_ge(stored[0], 32)
                copy(tokens(K_T[:, :]), group(0))
                copy(tokens(K_HI[:, :]), group(0)).then_inc(q_hi, 1)
                following(n0, 0, 1)
                done(n0, 0, 1)
                copy(tokens(V_T[:, :]), group(1)).then_inc(taken[1], 1)
                for m in range(NJ):
                    i, k = 1 + m // 2, m % 2
                    following(n0, i, k)
                    if m == 0:
                        act.wait_ge(rows_t, r_c + 1)
                        copy(KS[:, 0:PAST], PS[:, 6 + r_c % 2, 0:PAST]).then_inc(rows_out, 1)
                        rows_from(K_ROWS, k_tiles, r_c + 1, side)
                    if m == 2:
                        act.wait_ge(staged, 4 if side == 1 else 6)
                        rows_from(V_ROWS, TRIPLES, r_c + 1 + len(k_tiles), side)
                    done(n0, i, k)
                    copy(tokens(Q_HI[:, m, :]), group(k)).then_inc(q_hi, 1)

            def rows_from(dst, tiles, r, side):
                for m, (a, b) in enumerate(tiles):
                    act.wait_ge(rows_t, r + m + 1)
                    bank = 6 + (r + m) % 2
                    if b - a == 2:
                        copy(dst[:, a, :], PS[:, bank, 0:P])
                        copy(dst[0:DEC, a + 1, :], PS[0:DEC, bank, P:2 * P]).then_inc(rows_out, 1)
                        continue
                    n = rows_of(a)
                    src = PS[0:n, bank, 0:(b - a) * P].rearrange("p (t d) -> p t d", d=P)
                    if dst is V_ROWS and n == P:
                        copy(V_HI[:, a:b, :], src).then_inc(v_hi, 1)
                        act.wait_ge(v_lo, 2 * (side - 1) + m + 1)
                    elif dst is V_ROWS:
                        copy(VS[0:n, :], src[:, 0, :])
                    copy(dst[0:n, a:b, :], src).then_inc(rows_out, 1)

            def exp(pair, h):
                x, ub = pair["x"], pair["ub"]
                act.wait_ge(negated, 2 * x + (2 if pair["window"] else h + 1))
                p = probs_of(pair, h)
                nc.scalar.activation(p, p, ACT.Exp, bias=stat[:, ub, 1, h:h + 1],
                                     accum_out=stat[:, ub, 2, h:h + 1]).then_inc(exp_done, 1)
                if h == 1 and pair["window"]:
                    act.wait_ge(sink_shift, x + 1)
                    nc.scalar.activation(stat[:, ub, 4, :], stat[:, ub, 3, :], ACT.Exp).then_inc(sink_exp, 1)

            def normalise(pair, h):
                if pair["window"] and h == 0:
                    return
                act.wait_ge(inverse, 2 * pair["x"] + h + 1)
                p = probs_of(pair, h)
                nc.scalar.activation(p, p, ACT.Copy, scale=stat[:, pair["ub"], 5, h:h + 1]).then_inc(probs[h], 1)

            def pt_high(pair, c):
                q = pair["q"] + c
                act.wait_ge(pt_done, q + 1)
                if q >= 2:
                    act.wait_ge(pv_done, q - 1)
                if pair["sample"]:
                    rows = DEC if c == 1 else P
                    copy(PT_S[0:rows, q % 2, 0:P], PS[0:rows, 4 + q % 2, 0:P]).then_inc(pt_hi, 1)
                else:
                    n = 2 * P * len(pair["chunks"][c])
                    copy(PT_HI[:, q % 2, 0:n], PS[:, 4 + q % 2, 0:n]).then_inc(pt_hi, 1)

            def output(pair):
                act.wait_ge(pv_done, pair["q"] + len(pair["chunks"]))
                for g in groups_of(pair):
                    src, high, _ = attn_sums(pair, g)
                    last = copy(high, src)
                last.then_inc(o_hi, 1)

            def attend(ps):
                for pair in ps[0:2]:
                    exp(pair, 0)
                    exp(pair, 1)
                normalise(ps[0], 0)
                normalise(ps[0], 1)
                for y, pair in enumerate(ps):
                    ahead, count = front(ps, y), len(pair["chunks"])
                    after = ps[y + 1] if y + 1 < len(ps) else None
                    for c in range(max(count, 4)):
                        if c < count:
                            pt_high(pair, c)
                        if c < 2 and ahead:
                            exp(ahead, c)
                        if 1 <= c <= 2 and after:
                            normalise(after, c - 1)
                    if y > 0 and ps[y - 1]["last"]:
                        output(ps[y - 1])
                output(ps[-1])

            attention_jobs(J_B, 1, R_B_C, K_LAST)
            attend(WINDOW)
            act.wait_ge(stored[1], 16 * 6)
            gates(J_GB)
            attention_jobs(J_C, 2, R_C_C, TRIPLES)
            attend(SPARSE)
            act.wait_ge(stored[2], 16 * 4)
            gates(J_GC, merged=True)

            following(J_WO, 0, 0)
            for i in range(NT + 1):
                if i == 3:
                    following(J_WO, 0, 1)
                r = rows_of(i)
                act.wait_ge(xr_t, i + 1)
                src = PS[:, 6:8, :].rearrange("p b (j t) -> p (b j) t", t=P)
                copy(X2[:, :, i * P:i * P + r], src[:, :, 0:r]).then_inc(xr_out, 1)
            def residual(i, k):
                j = 2 * i + k
                act.wait_ge(taken[k], J_WO // 2 + i + 1)
                apart(act)
                nc.scalar.activation(tile_at(G_HI, j), tile_at(X2, j), ACT.Copy,
                                     scale=vec_at(j, V_NORM)).then_inc(g_hi, 1)
                act.wait_ge(ssq_sum, j + 1)
                apart(act)
                nc.scalar.activation(tokens(T1[:, 0:TOK]), tile_at(X2, j), ACT.Square).then_inc(res_sq, 1)

            residual(0, 0)
            residual(0, 1)
            with act.Fori(1, KT // 2) as i:
                for k in range(2):
                    following(J_WO, i, k)
                    residual(i, k)

            def ffn(g, f, f0):
                following(J_FFN[g], f, 0)
                act.wait_ge(conv_out, f + (f0 + 1))
                nc.scalar.activation(T0[:, 0:SEQ], T1[:, 0:SEQ], ACT.Silu)
                nc.scalar.activation(T0[:, SEQ:TOK], T1[:, SEQ + 2:TOK + 2], ACT.Silu).then_inc(silu_done, 1)
                following(J_FFN[g], f, 1)
                act.wait_ge(taken[1], J_FFN[g] // 2 + f + 1)
                apart(act)
                copy(tile_at(F_HI, f), tokens(T0[:, 0:TOK])).then_inc(f_hi, 1)

            f0 = 0
            for g, nf in enumerate(FFN_GROUPS):
                if g == 0:
                    ffn(0, 0, 0)
                with act.Fori(1 if g == 0 else 0, nf) as f:
                    ffn(g, f, f0)
                last_group = g == len(FFN_GROUPS) - 1
                count = KT // 2
                with act.Fori(0, count - 1 if last_group else count) as i:
                    following(J_DOWN[g], i, 0)
                    following(J_DOWN[g], i, 1)
                if last_group:
                    following(J_DOWN[g], count - 1, 0)
                f0 += nf
            act.wait_ge(state_t, 1)
            copy(U[0:N_COLS, 0:P], PS[0:N_COLS, 6, 0:P]).then_inc(state_out, 1)
            for i in range(NT + 1):
                r = rows_of(i)
                act.wait_ge(y_t, i + 1)
                if i >= 1:
                    act.wait_ge(y_sq, i)
                nc.scalar.activation(YJ[0:r, :],
                                     PS[0:r, 2 * (i % 3):2 * (i % 3) + 2, :].rearrange("p b n -> p (b n)"),
                                     ACT.Square, accum_out=ss[0:r, 0, i:i + 1]).then_inc(y_sq, 1)

        @block.vector
        def _(dve):
            step = Steps(dve, vector_step)
            V_ = nc.vector

            def split(n0, i, k):
                dve.wait_ge(hi_ready, n0 + 2 * i + k + 1)
                V_.tensor_tensor(WLO[:, k, :, :], RAW[:, k, :, :], WHI[:, k, :, :].bitcast(F32),
                                 ALU.subtract).then_inc(lo_ready, 1)

            def following(n0, i, k):
                split(n0, i, 1) if k == 0 else split(n0, i + 1, 0)

            def done(n0, i, k):
                dve.wait_ge(job_done, n0 + 2 * i + k + 1)

            def rsqrt(rows, var, power, power_done, n):
                dve.wait_ge(power_done, n)
                t = ss[0:rows, 0, 0:var.shape[1]]
                if var.shape[1] <= 3:
                    t = ss[0:rows, 3, 12 - var.shape[1]:12]
                step.mark(V_.tensor_tensor(t, power, power, ALU.mult))
                step.wait()
                step.mark(V_.tensor_tensor(t, t, var, ALU.mult))
                step.wait()
                step.mark(V_.tensor_scalar(t, t, -0.5, 1.5, ALU.mult, ALU.add))
                step.wait()
                return V_.tensor_tensor(power, power, t, ALU.mult)

            step.mark(V_.memset(SS[:, :], 1.0))
            step.wait()
            V_.memset(ss[:, 3, 0:1], -0.5).then_inc(ss_clear, 1)
            step.mark(V_.memset(MASK0[:, :], 0.0))
            step.mark(V_.memset(MASKW[:, :], 0.0))
            step.wait()
            V_.memset(MASK0[0:CHUNK, 2 * P - CHUNK:2 * P], NEG)
            V_.memset(MASKW[0:CHUNK, 2 * P - CHUNK:2 * P], NEG)
            V_.memset(MASKW[CHUNK:P, 0:CHUNK], NEG)
            dve.wait_ge(misc_in, 16 * 7)
            for j in range(NJ):
                V_.tensor_copy(SINK_S[DEC * j:DEC * (j + 1), :], SINK[DEC * j:DEC * (j + 1), j:NH:NJ])
                V_.tensor_scalar(NEG_SINK[DEC * j:DEC * (j + 1), NH:NH + NKV],
                                 SINK[DEC * j:DEC * (j + 1), j:NH:NJ], -1.0, None, ALU.mult)
            step.mark(V_.tensor_scalar(NEG_SINK[:, 0:NH], SINK[:, :], -1.0, None, ALU.mult))
            step.wait()

            def h_low(i):
                r = rows_of(i)
                dve.wait_ge(h_hi, i + 1)
                src = PS[:, 2 * (i % 3):2 * (i % 3) + 2, :].rearrange("p b (j t) -> p (b j) t", t=P)[:, :, 0:r]
                V_.tensor_tensor(H_LO[:, :, i * P:i * P + r], src,
                                 H_HI[:, :, i * P:i * P + r].bitcast(F32), ALU.subtract).then_inc(h_lo, 1)

            done_low = 0
            for m in range((NT + 1) // 3):
                var, power = ss[:, 1, 3 * m:3 * m + 3], ss[:, 2, 3 * m:3 * m + 3]
                dve.wait_ge(x_sq, 3 * m + 3)
                V_.tensor_scalar(var, ss[:, 0, 3 * m:3 * m + 3], 1.0 / D, EPS, ALU.mult, ALU.add).then_inc(x_var, 1)
                dve.wait_ge(x_var, m + 1)
                step.mark(rsqrt(P, var, power, x_pow, m + 1))
                step.wait()
                for i in range(3 * m, 3 * m + 3):
                    r = rows_of(i)
                    if i >= 3:
                        dve.wait_ge(h_t, i - 2)
                    V_.scalar_tensor_tensor(HN[0:r, i % 3, :], XIN[0:r, i, :], ss[0:r, 2, i:i + 1],
                                            NG[0:r, :], ALU.mult, ALU.mult).then_inc(h_rows, 1)
                    if i >= 2:
                        h_low(i - 2)
                        done_low += 1
            for i in range(done_low, NT + 1):
                h_low(i)

            split(0, 0, 0)
            for n in range(4):
                following(J_IDX, n // 2, n % 2)
            dve.wait_ge(taken[1], 2)
            V_.tensor_copy(WS[:, :].rearrange("p (r t) -> p r t", t=DEC),
                           WIT[:, SEQ:TOK].unsqueeze(1).broadcast_to([IDXH, 4, DEC])).then_inc(staged, 1)
            for t in range(2):
                last = V_.tensor_copy(QS2[:, t, :].rearrange("p (r t) -> p r t", t=DEC),
                                      QI[:, t, SEQ:TOK].unsqueeze(1).broadcast_to([P, 4, DEC]))
            last.then_inc(staged, 1)
            dve.wait_ge(taken[0], 2)
            dve.wait_ge(rows_out, R_IDX_C + 1)
            V_.tensor_copy(KSI[:, PAST:PAST + DEC], KI[:, SEQ:TOK]).then_inc(staged, 1)

            def score(i):
                return MASK[:, SEL_AT[i]:SEL_AT[i] + (i + 1) * P] if i < NT else MASK_S[:, :]

            dve.wait_ge(rows_out, R_IDX_W + 1)
            c = 0
            for i in SEL + [NT]:
                s = score(i)
                n = s.shape[1]
                for h in range(IDXH):
                    w = WI[:, IDXH * i + h:IDXH * i + h + 1]
                    dve.wait_ge(idx_relu, c + 1)
                    if h == 0:
                        V_.tensor_scalar(s, S_SB[:, c % 2, 0:n], w, None, ALU.mult).then_inc(idx_sum, 1)
                    else:
                        dve.wait_ge(idx_sum, c)
                        V_.scalar_tensor_tensor(s, S_SB[:, c % 2, 0:n], w, s, ALU.mult,
                                                ALU.add).then_inc(idx_sum, 1)
                    c += 1
                if i < NT:
                    dve.wait_ge(idx_sum, c)
                    step.mark(V_.memset(s[0:CHUNK, n - CHUNK:n], NEG))
            step.wait()

            def select(i, rounds):
                s = score(i)
                for _ in range(rounds):
                    apart(dve)
                    step.mark(V_.max(TOP8[:, :], s))
                    step.wait()
                    apart(dve)
                    step.mark(V_.match_replace(s, TOP8[:, :], s, TAKEN))
                    step.wait()

            def to_mask(i):
                step.mark(V_.tensor_scalar(score(i), score(i), TAKEN, NEG, ALU.not_equal, ALU.mult))
                step.wait()

            def conv_input(k, other):
                full = 2 * PIECE
                V_.tensor_tensor(U[:, 2:2 + full].rearrange("p (b n) -> p b n", b=2),
                                 PS[:, NB * k:NB * k + 2, 0:PIECE],
                                 other[:, 0:full].rearrange("p (b n) -> p b n", b=2), ALU.mult)
                V_.tensor_tensor(U[:, 2 + full:2 + SEQ], PS[:, NB * k + 2, 0:SEQ - full],
                                 other[:, full:SEQ], ALU.mult)
                V_.tensor_tensor(U[:, SEQ + 4:TOK + 4], PS[:, NB * k + 2, SEQ - full:PIECE],
                                 other[:, SEQ:TOK], ALU.mult).then_inc(taken[k], 1)

            def states(t, width, at_state, at_new):
                old = VEC[:, VEC_ROWS + at_state:VEC_ROWS + at_state + 2 * width].rearrange("p (s t) -> p s t", s=2)
                new = NEW[:, at_new:at_new + 4 * width].rearrange("p (s t) -> p s t", s=4)
                V_.tensor_copy(new[:, 0:2, bass.ds(t, 1)], U[:, SEQ:SEQ + 2].unsqueeze(2))
                V_.tensor_copy(new[:, 2:4, bass.ds(t, 1)], U[:, TOK + 2:TOK + 4].unsqueeze(2))
                step.mark(V_.tensor_copy(U[:, SEQ + 2:SEQ + 4].unsqueeze(2), old[:, :, bass.ds(t, 1)]))
                step.wait()

            def convolve(taps, out):
                n = TOK + 2
                step.mark(V_.tensor_scalar(out[:, 0:n], U[:, 0:n], taps[0], None, ALU.mult))
                for w in (1, 2):
                    step.wait()
                    last = V_.scalar_tensor_tensor(out[:, 0:n], U[:, w:n + w], taps[w], out[:, 0:n],
                                                   ALU.mult, ALU.add)
                    if w == 1:
                        step.mark(last)
                return last

            V_.memset(U[:, 0:2], 0.0).then_inc(a_lo, 1)
            dve.wait_ge(tables_ready, 1)
            ROUNDS = TOPK // 8
            with dve.Fori(0, CT // 2) as i:
                with step.loop(i, CT // 2, 2 * (1 + 3) + 2 * (ROUNDS // 2)):
                    for m in range(6):
                        n0, k, t = J_A + 2 * (m // 2), m % 2, m // 3
                        following(n0, 3 * i, k)
                        if m % 3 != 2:
                            select(SEL[3], ROUNDS // 8)
                            continue
                        done(n0, 3 * i, k)
                        dve.wait_ge(taken[1 - k], J_A // 2 + 3 * i + (m - 1) // 2 + 1)
                        conv_input(k, T1)
                        dve.wait_ge(taken[k], n0 // 2 + 3 * i + 1)
                        states(2 * i + t, CT, S_CA, N_CA)
                        step.mark(convolve([vec_at(2 * i + t, V_CA + w * CT) for w in range(3)], T3))
                        step.wait()
                        V_.tensor_tensor(T1[:, 0:SEQ], T3[:, 0:SEQ], T0[:, 0:SEQ], ALU.mult)
                        V_.tensor_tensor(T1[:, SEQ:TOK], T3[:, SEQ + 2:TOK + 2], T0[:, SEQ:TOK],
                                         ALU.mult).then_inc(a_sum, 1)
                        dve.wait_ge(a_hi, 2 * i + t + 1)
                        V_.tensor_tensor(tile_at(A_LO, 2 * i + t), tokens(T1[:, 0:TOK]),
                                         tile_at(A_HI, 2 * i + t).bitcast(F32),
                                         ALU.subtract).then_inc(a_lo, 1)

            def gates(n0, mode, i, rounds, more=0):
                with dve.Fori(0, KT) as j:
                    with step.loop(j, KT, 2 * (rounds + more)):
                        following(n0, j, 0)
                        select(i, rounds)
                        select(SEL[0], more)
                        following(n0, j, 1)
                        done(n0, j, 1)
                        dve.wait_ge(taken[0], n0 // 2 + j + 1)
                        gate = tokens(T0[:, 0:TOK])
                        acc = tile_at(MACC, j)
                        if mode == "first":
                            V_.tensor_tensor(acc, group(1), gate, ALU.mult).then_inc(taken[1], 1)
                        else:
                            V_.tensor_tensor(tokens(T1[:, 0:TOK]), group(1), gate, ALU.mult).then_inc(taken[1], 1)
                            dve.wait_ge(taken[1], n0 // 2 + j + 1)
                            out = acc if mode == "middle" else tokens(T3[:, 0:TOK])
                            last = V_.tensor_tensor(out, acc, tokens(T1[:, 0:TOK]), ALU.add)
                            if mode == "last":
                                last.then_inc(sum_ready, 1)
                                dve.wait_ge(m_hi, j + 1)
                                V_.tensor_tensor(tile_at(M_LO, j), tokens(T3[:, 0:TOK]),
                                                 tile_at(M_HI, j).bitcast(F32),
                                                 ALU.subtract).then_inc(m_lo, 1)

            def attention_jobs(n0, i, side, r_v):
                heads = (NJ + 1) * (side - 1)
                rounds = ROUNDS // (NJ + 2)

                def low(n, out, high):
                    dve.wait_ge(q_hi, heads + n + 1)
                    V_.tensor_tensor(out, group(k), high.bitcast(F32), ALU.subtract).then_inc(taken[k], 1)

                for m in range(NJ + 2):
                    k = m % 2
                    following(n0, m // 2, k)
                    if m == 2:
                        dve.wait_ge(rows_out, (R_B_C if side == 1 else R_C_C) + 1)
                        V_.tensor_copy(KS[:, PAST:PAST + DEC], K_T[:, SEQ:TOK]).then_inc(staged, 1)
                    if m == 4:
                        for y, (a, b) in enumerate(TRIPLES[:2]):
                            dve.wait_ge(v_hi, 2 * (side - 1) + y + 1)
                            src = PS[:, 6 + (r_v + y) % 2, 0:(b - a) * P].rearrange("p (t d) -> p t d", d=P)
                            V_.tensor_tensor(V_LO[:, a:b, :], src, V_HI[:, a:b, :].bitcast(F32),
                                             ALU.subtract).then_inc(v_lo, 1)
                    select(i, rounds if m < NJ + 1 else ROUNDS - (NJ + 1) * rounds)
                    if m == NJ + 1:
                        to_mask(i)
                    if m == 0:
                        low(0, tokens(K_LO[:, :]), tokens(K_HI[:, :]))
                    elif m > 1:
                        low(m - 1, tokens(Q_LO[:, m - 2, :]), tokens(Q_HI[:, m - 2, :]))
                for k in range(2):
                    dve.wait_ge(taken[k], n0 // 2 + 3)
                V_.tensor_tensor(QS[:, :].rearrange("p (j t) -> p j t", t=DEC),
                                 Q_HI[:, :, SEQ:TOK].bitcast(F32), Q_LO[:, :, SEQ:TOK].bitcast(F32),
                                 ALU.add).then_inc(staged, 1)

            def mask_max(pair, h):
                x, ub, n, window = pair["x"], pair["ub"], pair["n"], pair["window"]
                dve.wait_ge(s_done, 2 * x + h + 1)
                if h == 0 and pair["free"]:
                    dve.wait_ge(pt_done, pair["free"])
                if h == 0 and not window and not pair["sample"] and pair["x"] == SPARSE[1]["x"]:
                    dve.wait_ge(stored[2], 16 * 4)
                top, neg = stat[:, ub, 0, h:h + 1], stat[:, ub, 1, h:h + 1]
                out = probs_of(pair, h)
                if pair["mask"] is None:
                    V_.tensor_scalar(out, scores_of(pair, h), SCALE, None, ALU.mult, ALU.max,
                                     accum_out=top).then_inc(masked, 1)
                else:
                    V_.tensor_tensor_reduce(out=out, in0=scores_of(pair, h), in1=pair["mask"], scale=SCALE,
                                            scalar=-3.4e38, op0=ALU.add, op1=ALU.max,
                                            accum_out=top).then_inc(masked, 1)
                if not window:
                    dve.wait_ge(masked, 2 * x + h + 1)
                    V_.tensor_scalar(neg, top, -1.0, None, ALU.mult).then_inc(negated, 1)

            def invert(pair, h):
                x, ub = pair["x"], pair["ub"]
                dve.wait_ge(exp_done, 2 * x + h + 1)
                V_.reciprocal(stat[:, ub, 5, h:h + 1], stat[:, ub, 2, h:h + 1]).then_inc(inverse, 1)

            def window_stats(ahead, after):
                if after:
                    dve.wait_ge(sink_exp, after["x"] + 1)
                    den, inv = stat[:, after["ub"], 2, :], stat[:, after["ub"], 5, :]
                    step.mark(V_.tensor_tensor(den, den, stat[:, after["ub"], 4, :], ALU.add))
                if ahead:
                    x, ub = ahead["x"], ahead["ub"]
                    dve.wait_ge(masked, 2 * x + 2)
                    V_.scalar_tensor_tensor(stat[:, ub, 1, :], stat[:, ub, 0, :], -1.0, ahead["negative"],
                                            ALU.mult, ALU.min).then_inc(negated, 2)
                if after:
                    step.wait()
                    V_.reciprocal(inv, den).then_inc(inverse, 2)
                if ahead:
                    dve.wait_ge(negated, 2 * x + 2)
                    V_.tensor_tensor(stat[:, ub, 3, :], stat[:, ub, 1, :], ahead["sinks"],
                                     ALU.add).then_inc(sink_shift, 1)
                if after:
                    dve.wait_ge(inverse, 2 * after["x"] + 2)
                    p = probs_of(after, 0)
                    V_.tensor_scalar(p, p, inv[:, 0:1], None, ALU.mult).then_inc(probs[0], 1)

            def pt_low(pair, c):
                q = pair["q"] + c
                if pair["sample"]:
                    rows = DEC if c == 1 else P
                    dve.wait_ge(pt_hi, q + 1)
                    V_.tensor_copy(PT_S[0:rows, q % 2, P:2 * P], PS[0:rows, 4 + q % 2, P:2 * P]).then_inc(pt_lo, 1)
                else:
                    n = 2 * P * len(pair["chunks"][c])
                    dve.wait_ge(pt_hi, q + 1)
                    V_.tensor_tensor(PT_LO[:, q % 2, 0:n], PS[:, 4 + q % 2, 0:n],
                                     PT_HI[:, q % 2, 0:n].bitcast(F32), ALU.subtract).then_inc(pt_lo, 1)

            def output(pair):
                dve.wait_ge(o_hi, pair["o"] + 1)
                for g in groups_of(pair):
                    src, high, out = attn_sums(pair, g)
                    last = V_.tensor_tensor(out, src, high.bitcast(F32), ALU.subtract)
                last.then_inc(o_lo, 1)

            def attend(ps):
                window = ps[0]["window"]
                for pair in ps[0:2]:
                    mask_max(pair, 0)
                    mask_max(pair, 1)
                    if window:
                        window_stats(pair, None)
                if window:
                    window_stats(None, ps[0])
                else:
                    invert(ps[0], 0)
                    invert(ps[0], 1)
                for y, pair in enumerate(ps):
                    ahead, count = front(ps, y), len(pair["chunks"])
                    after = ps[y + 1] if y + 1 < len(ps) else None
                    if ahead:
                        mask_max(ahead, 0)
                        if window:
                            mask_max(ahead, 1)
                    if window:
                        window_stats(ahead, after)
                    for c in range(max(count, 4)):
                        if c < count:
                            pt_low(pair, c)
                        if c == 0 and ahead and not window:
                            mask_max(ahead, 1)
                        if 1 <= c <= 2 and after and not window:
                            invert(after, c - 1)
                    if y > 0 and ps[y - 1]["last"]:
                        output(ps[y - 1])
                output(ps[-1])

            to_mask(SEL[3])
            gates(J_GA, "first", SEL[5], ROUNDS // KT, ROUNDS // KT // 2)
            to_mask(SEL[5])
            select(NT, TOPK_S // 8)
            to_mask(NT)
            attention_jobs(J_B, SEL[2], 1, R_B_V)
            attend(WINDOW)
            dve.wait_ge(stored[1], 16 * 6)
            gates(J_GB, "middle", SEL[4], ROUNDS // KT, ROUNDS // KT // 2)
            to_mask(SEL[4])
            to_mask(SEL[0])
            attention_jobs(J_C, SEL[1], 2, R_C_V)
            attend(SPARSE)
            gates(J_GC, "last", SEL[0], 0)

            V_.memset(T0[:, 0:TOK], 0.0).then_inc(ssq_sum, 1)
            V_.memset(U[:, 0:2], 0.0)
            following(J_WO, 0, 0)
            following(J_WO, 0, 1)
            dve.wait_ge(xr_out, NT + 1)

            def residual(i, k):
                    j = 2 * i + k
                    done(J_WO, i, k)
                    V_.tensor_tensor(tile_at(X2, j), group(k), tile_at(X2, j), ALU.add).then_inc(taken[k], 1)
                    dve.wait_ge(taken[k], J_WO // 2 + i + 1)
                    dve.wait_ge(g_hi, j + 1)
                    V_.scalar_tensor_tensor(tile_at(G_LO, j), tile_at(X2, j), vec_at(j, V_NORM),
                                            tile_at(G_HI, j).bitcast(F32), ALU.mult,
                                            ALU.subtract).then_inc(g_lo, 1)
                    dve.wait_ge(res_sq, j + 1)
                    dve.wait_ge(ssq_sum, j + 1)
                    V_.tensor_tensor(T0[:, 0:TOK], T0[:, 0:TOK], T1[:, 0:TOK], ALU.add).then_inc(ssq_sum, 1)

            residual(0, 0)
            residual(0, 1)
            with dve.Fori(1, KT // 2) as i:
                for k in range(2):
                    following(J_WO, i, k)
                    residual(i, k)

            def second_norm():
                dve.wait_ge(ss_done, 1)
                V_.tensor_scalar(ss[0:96, 1, 0:11], PS[0:96, 6, 0:11], 1.0 / D, EPS,
                                 ALU.mult, ALU.add).then_inc(ss_var, 1)
                dve.wait_ge(ss_var, 1)
                rsqrt(96, ss[0:96, 1, 0:11], ss[0:96, 2, 0:11], ss_pow, 1).then_inc(ss_rstd, 1)
                for m in range(3):
                    a, b = 480 * m, min(480 * (m + 1), TOK)
                    dve.wait_ge(rb_done, m + 1)
                    V_.tensor_copy(T3[:, a:b], PS[:, 7 - m % 2, 0:b - a]).then_inc(rb_ready, 1)
                dve.wait_ge(rb_ready, 3)

            def ffn(g, f, f0):
                following(J_FFN[g], f, 0)
                if g == 0 and isinstance(f, int):
                    second_norm()
                done(J_FFN[g], f, 0)
                conv_input(0, T3)
                dve.wait_ge(taken[0], J_FFN[g] // 2 + f + 1)
                states(f + f0, FT, S_CF, N_CF)
                convolve([vec_at(f, V_CF + w * FT + f0) for w in range(3)], T1).then_inc(conv_out, 1)
                following(J_FFN[g], f, 1)
                done(J_FFN[g], f, 1)
                dve.wait_ge(silu_scaled, f + (f0 + 1))
                V_.tensor_tensor(tokens(T0[:, 0:TOK]), group(1), tokens(T0[:, 0:TOK]),
                                 ALU.mult).then_inc(taken[1], 1)
                dve.wait_ge(f_hi, f + (f0 + 1))
                V_.tensor_tensor(tile_at(F_LO, f), tokens(T0[:, 0:TOK]), tile_at(F_HI, f).bitcast(F32),
                                 ALU.subtract).then_inc(f_lo, 1)

            def down(g, i, k, more=True):
                if more:
                    following(J_DOWN[g], i, k)
                done(J_DOWN[g], i, k)
                j = 2 * i + k
                V_.tensor_tensor(tile_at(X2, j), group(k), tile_at(X2, j), ALU.add).then_inc(taken[k], 1)

            f0 = 0
            for g, nf in enumerate(FFN_GROUPS):
                if g == 0:
                    ffn(0, 0, 0)
                with dve.Fori(1 if g == 0 else 0, nf) as f:
                    if g == 0:
                        with step.loop(f - 1, nf - 1, 3):
                            ffn(g, f, f0)
                    else:
                        with step.loop(f, nf, 3):
                            ffn(g, f, f0)
                last_group = g == len(FFN_GROUPS) - 1
                with dve.Fori(0, KT // 2 - 1 if last_group else KT // 2) as i:
                    for k in range(2):
                        down(g, i, k)
                if last_group:
                    down(g, KT // 2 - 1, 0)
                    down(g, KT // 2 - 1, 1, more=False)
                f0 += nf

            dve.wait_ge(nf_in, 16)
            for i in range(NT + 1):
                r = rows_of(i)
                dve.wait_ge(y_sq, i + 1)
                V_.tensor_scalar(ss[0:r, 1, i:i + 1], ss[0:r, 0, i:i + 1], 1.0 / D, EPS,
                                 ALU.mult, ALU.add).then_inc(y_var, 1)
                dve.wait_ge(y_var, i + 1)
                step.mark(rsqrt(r, ss[0:r, 1, i:i + 1], ss[0:r, 2, i:i + 1], y_pow, i + 1))
                step.wait()
                if i >= 3:
                    dve.wait_ge(y_out[i % 3], 16 * (i // 3))
                V_.scalar_tensor_tensor(Y[0:r, i % 3, :],
                                        PS[0:r, 2 * (i % 3):2 * (i % 3) + 2, :].rearrange("p b n -> p (b n)"),
                                        ss[0:r, 2, i:i + 1], NF[0:r, :], ALU.mult, ALU.mult).then_inc(y_ready, 1)


_INS = ["x_prompt", "x_sample", "state_conv_a", "cache_swa_k", "cache_swa_v", "cache_dsa_k", "cache_dsa_v",
        "cache_idx_k", "state_ffn_conv", "norm_mix", "w_in", "conv_a", "w_a_out", "attn_sinks", "w_swa_o",
        "w_dsa_o", "w_out", "norm_ffn", "w_gate", "w_up", "conv_ffn", "w_down", "norm_final"]
_OUTS = [(1, SEQ, D), (1, DEC, D),
         (1, 1, 2, D_CONV), (1, 1, P, NKV, HD), (1, 1, P, NKV, HD), (1, 1, SEQ, NKV, HD), (1, 1, SEQ, NKV, HD),
         (1, 1, SEQ, HD), (1, 1, 2, D_FF),
         (1, 1, 2, D_CONV), (1, 1, P, NKV, HD), (1, 1, P, NKV, HD), (1, 1, DEC, NKV, HD), (1, 1, DEC, NKV, HD),
         (1, 1, DEC, HD), (1, 1, 2, D_FF)]


def kernel(**inputs):
    import numpy as _np
    import concourse.bacc as _bacc
    from concourse import mybir as _mybir
    from concourse.bass_utils import run_bass_kernel_spmd as _run

    nc = _bacc.Bacc("TRN2", target_bir_lowering=False, num_devices=1, dynamic_dma_scratch_size=4096)
    arrays, ins = {}, {}
    for name in _INS:
        a = _np.ascontiguousarray(inputs[name])
        arrays[f"in_{name}"] = a
        ins[name] = nc.dram_tensor(f"in_{name}", a.shape, _mybir.dt.from_np(a.dtype), kind="ExternalInput").ap()
    outs = [nc.dram_tensor(f"out_{i}", shape, _mybir.dt.float32, kind="ExternalOutput").ap()
            for i, shape in enumerate(_OUTS)]
    build(nc, ins, outs)
    r = _run(nc, [arrays], core_ids=[0])
    return tuple(r.results[0][f"out_{i}"] for i in range(len(_OUTS)))
```

```python
from contextlib import ExitStack, contextmanager

import concourse.bass as bass
from concourse import mybir

ALU = mybir.AluOpType
ACT = mybir.ActivationFunctionType
F32 = mybir.dt.float32
F32R = mybir.dt.float32r

P = 128
D = 1024
KT = D // P
SEQ, DEC = 1024, 32
TOK = SEQ + DEC
BANK = 512
NB = 3
PIECE = TOK // NB
NT = SEQ // P
D_CONV = 512
CT = D_CONV // P
HD = 64
NH, NKV = 8, 2
NJ = NH // NKV
PAST = 128
CHUNK = 64
TOPK, TOPK_S = 256, (PAST + DEC) // 4
IDXH = 4
D_FF = 2816
FT = D_FF // P
FFN_GROUPS = (8, 8, 6)
EPS = 1e-6
NEG = -1e30
TAKEN = -3.0e38
SCALE = HD ** -0.5

C_AB, C_AC, C_AX = 0, 512, 1024
C_QB, C_KB, C_VB = 1536, 2048, 2176
C_QC, C_KC, C_VC = 2304, 2816, 2944
C_QI, C_KI, C_WI = 3072, 3328, 3392
C_G = 3396

J_IDX = 0
J_A = J_IDX + 4
J_GA = J_A + 3 * CT
J_B = J_GA + 2 * KT
J_GB = J_B + NJ + 2
J_C = J_GB + 2 * KT
J_GC = J_C + NJ + 2
J_WO = J_GC + 2 * KT
J_FFN = []
J_DOWN = []
_n = J_WO + KT
for _g in FFN_GROUPS:
    J_FFN.append(_n)
    J_DOWN.append(_n + 2 * _g)
    _n += 2 * _g + KT
J_END = _n

V_NORM, V_CA, V_CF = 0, KT, KT + 3 * CT
V_NF = V_CF + 3 * FT
VEC_ROWS = V_NF + KT
S_CA, S_CF = 0, 2 * CT
S_ROWS = S_CF + 2 * FT
N_CA, N_CF = 0, 4 * CT
N_COLS = N_CF + 4 * FT

SEL = [i for i in range(NT) if (i + 1) * P > TOPK]
SEL_AT = {}
_at = 0
for _i in SEL:
    SEL_AT[_i] = _at
    _at += (_i + 1) * P
SEL_COLS = _at


def rows_of(i):
    return P if i < NT else DEC


def apart(eng):
    eng.nop(nofuse=True)


class Steps:

    def __init__(self, eng, sem):
        self.eng, self.sem, self.n, self.marked = eng, sem, 0, 0

    def mark(self, instruction):
        instruction.then_inc(self.sem, 1)
        self.n, self.marked = self.n + 1, self.marked + 1
        return instruction

    def wait(self, mark=None):
        back = 0 if mark is None else self.marked - mark
        self.eng.wait_ge(self.sem, self.n if back == 0 else self.n - back)

    @contextmanager
    def loop(self, i, count, per):
        start, marked = self.n, self.marked
        self.n = i * per + start
        yield
        assert self.marked - marked == per, (self.marked - marked, per)
        self.n = start + count * per


def build(nc, ins, outs):
    with ExitStack() as ctx:
        def sem(name):
            return ctx.enter_context(nc.semaphore(name))

        base = (nc.sbuf_base + 63) // 64 * 64
        UNIT = 4 * TOK

        def place(name, shape, dt, units, extra=0):
            return nc.alloc_sbuf_tensor_at(name, shape, dt, offset=base + int(units * UNIT) + extra)

        H_HI = place("h_hi", [P, KT, TOK], F32R, 0)
        X2 = place("residual", [P, KT, TOK], F32, 0)
        H_LO = place("h_lo", [P, KT, TOK], F32R, 8)
        G_HI = place("h2_hi", [P, KT, TOK], F32R, 8)
        XG = place("y_columns", [P, KT, TOK], F32, 8)
        MACC = place("merge_sum", [P, KT, TOK], F32, 16)
        M_HI = place("merged_hi", [P, KT, TOK], F32R, 16)
        F_HI = place("ffn_hi", [P, KT, TOK], F32R, 16)
        HN = place("h_rows", [P, 3, D], F32, 16)
        NG = place("norm_mix_rows", [P, D], F32, 16, 3 * 4 * D)
        XJ = place("x_squares", [P, D], F32, 16, 4 * 4 * D)
        XIN = place("x_rows", [P, NT + 1, D], F32, 24)
        Y = place("y", [P, NT + 1, D], F32, 24)
        XR = place("x_rows_again", [P, NT + 1, D], F32, 24)
        A_HI = place("a_hi", [P, CT, TOK], F32R, 24)
        A_LO = place("a_lo", [P, CT, TOK], F32R, 28)
        QI = place("idx_q_parts", [P, IDXH, TOK], F32R, 24)
        KI = place("idx_k", [P, TOK], F32, 28)
        KI_HI = place("idx_k_hi", [P, TOK], F32R, 29)
        KI_LO = place("idx_k_lo", [P, TOK], F32R, 30)
        WIT = place("idx_w", [IDXH, TOK], F32, 31)
        Q_HI = place("q_hi", [P, NJ, TOK], F32R, 24)
        K_HI = place("k_hi", [P, TOK], F32R, 28)
        K_LO = place("k_lo", [P, TOK], F32R, 29)
        Q_LO = place("q_lo", [P, NJ, TOK], F32R, 30)
        O_HI = place("attn_hi", [P, NJ, TOK], F32R, 24)
        O_LO = place("attn_lo", [P, NJ, TOK], F32R, 30)
        G_LO = place("h2_lo", [P, KT, TOK], F32R, 24)
        MASK = place("key_mask", [P, SEL_COLS], F32, 34)
        S_SB = place("idx_scores", [P, 2, D], F32, 38, 4608)
        KI_ROWS = place("idx_k_rows", [P, NT + 1, HD], F32, 38, 4608 + 8192)
        M_LO = place("merged_lo", [P, KT, TOK], F32R, 34)
        F_LO = place("ffn_lo", [P, KT, TOK], F32R, 34)
        V_IN = place("vector_rows", [P, P], F32, 34)
        S_IN = place("state_rows", [P, P], F32, 34, 512)
        T0 = place("t0", [P, TOK + 4], F32, 42)
        T1 = place("t1", [P, TOK + 4], F32, 42, 4256)
        U = place("conv_in", [P, TOK + 4], F32, 42, 2 * 4256)
        T3 = place("t3", [P, TOK + 4], F32, 42, 3 * 4256)
        QS2 = place("sample_idx_q", [P, 2, P], F32, 42, 8704 + 1664)
        WS = place("sample_idx_w", [IDXH, P], F32, 42, 8704 + 2688)
        KSI = place("sample_idx_keys", [P, PAST + DEC], F32, 42, 8704)
        KCI = place("cache_idx_k_rows", [P, P], F32, 42, 8704 + 640)
        V_HI = place("v_hi", [P, NT, P], F32R, 38)
        V_LO = place("v_lo", [P, NT, P], F32R, 38, 4 * NT * P)
        PT_HI = place("probs_t_hi", [P, 2, BANK], F32R, 38, 8192)
        PT_LO = place("probs_t_lo", [P, 2, BANK], F32R, 38, 8192 + 4096)
        PT_S = place("probs_t_sample", [P, 2, BANK], F32, 38, 8192)
        K_T = place("k_columns", [P, TOK], F32, 38)
        V_T = place("v_columns", [P, TOK], F32, 38, 8192)
        PR = place("probs", [P, 4 * D], F32, 38, 16384)
        K_ROWS = place("k_rows", [P, NT + 1, P], F32, 38, 16384 + 2048)
        V_ROWS = place("v_rows", [P, NT + 1, P], F32, 38, 16384 + 2048 + 4608)
        KC = place("cache_k_rows", [P, P], F32, 38, 16384 + 2048 + 9216)
        KS = place("sample_k", [P, PAST + DEC], F32, 38, 32768)
        QS = place("sample_q", [P, P], F32, 38, 32768 + 640)
        wbase = 42 * UNIT + 4 * 4256
        RAW = place("w_raw", [P, 2, KT, P], F32, 0, wbase)
        WHI = place("w_hi", [P, 2, KT, P], F32R, 0, wbase + 8192)
        WLO = place("w_lo", [P, 2, KT, P], F32R, 0, wbase + 16384)
        top = wbase + 24576
        fixed = {}

        def keep(name, cols, rows=P):
            nonlocal top
            fixed[name] = place(name, [rows, cols], F32, 0, top)
            top += (4 * cols + 31) // 32 * 32
            return fixed[name]

        IDENT = keep("ident", P)
        ONES = keep("ones", 1)
        VEC = keep("vectors", VEC_ROWS + S_ROWS)
        NEW = keep("new_states", N_COLS)
        MASK0 = keep("mask_causal", 2 * P)
        MASKW = keep("mask_window", 2 * P)
        MASK_S = keep("mask_sample", PAST + DEC)
        WI = keep("idx_w_rows", IDXH * (NT + 1))
        SINK = keep("sinks", NH)
        SINK_S = keep("sinks_sample", NKV)
        TOP8 = keep("top8", 24)
        NEG_SINK = keep("sinks_negated", NH + NKV)
        STAT = keep("softmax_stats", 3 * 6 * 2)
        VC = keep("cache_v_rows", P)
        VS = keep("sample_v_rows", P)
        SS = keep("norm_stats", 4 * 12)
        assert base + top <= nc.sbuf_usable_end, (base + top, nc.sbuf_usable_end)
        stat = STAT[:, :].rearrange("p (u s h) -> p u s h", u=3, s=6)
        ss = SS[:, :].rearrange("p (s i) -> p s i", s=4)

        def vec_at(i, row):
            return VEC[:, bass.ds(i + row, 1)]

        PS = ctx.enter_context(nc.psum_tensor("ps", [P, 8, BANK], F32))

        raw_full = [sem("raw_full0"), sem("raw_full1")]
        hi_ready, lo_ready = sem("hi_ready"), sem("lo_ready")
        job_done = sem("job_done")
        taken = [sem("taken0"), sem("taken1")]
        x_in = [sem(f"x_in{k}") for k in range(NT + 1)]
        misc_in, x_sq, x_var, x_pow, h_rows, h_t, h_hi, h_lo = (
            sem(n) for n in ("misc_in", "x_sq", "x_var", "x_pow", "h_rows", "h_t", "h_hi", "h_lo"))
        const_ready, tables_t, tables_ready = sem("const_ready"), sem("tables_t"), sem("tables_ready")
        pool_step, vector_step = sem("pool_step"), sem("vector_step")
        rows_t, rows_out = sem("rows_t"), sem("rows_out")
        side_in = [sem("side_in_idx"), sem("side_in_b"), sem("side_in_c")]
        stored = [sem("stored_idx"), sem("stored_b"), sem("stored_c")]
        idx_hi = sem("idx_hi")
        staged = sem("staged")
        idx_s, idx_relu, idx_sum = sem("idx_s"), sem("idx_relu"), sem("idx_sum")
        a_sum, a_hi, a_lo = sem("a_sum"), sem("a_hi"), sem("a_lo")
        sum_ready, m_hi, m_lo = sem("sum_ready"), sem("m_hi"), sem("m_lo")
        q_hi = sem("q_hi")
        s_done, masked, negated, exp_done = sem("s_done"), sem("masked"), sem("negated"), sem("exp_done")
        sink_shift, sink_exp, inverse = sem("sink_shift"), sem("sink_exp"), sem("inverse")
        probs = [sem("probs_ready0"), sem("probs_ready1")]
        pt_done, pt_hi, pt_lo, pv_done = sem("pt_done"), sem("pt_hi"), sem("pt_lo"), sem("pv_done")
        v_hi, v_lo = sem("v_hi"), sem("v_lo")
        o_hi, o_lo = sem("o_hi"), sem("o_lo")
        xr_in = [sem(f"xr_in{k}") for k in range(NT // 2 + 1)]
        xr_t, xr_out = sem("xr_t"), sem("xr_out")
        g_hi, g_lo, res_sq, ssq_sum = sem("g_hi"), sem("g_lo"), sem("res_sq"), sem("ssq_sum")
        ss_done, ss_var, ss_pow, ss_rstd, rb_done, rb_ready = (
            sem(n) for n in ("ss_done", "ss_var", "ss_pow", "ss_rstd", "rb_done", "rb_ready"))
        conv_out, silu_done, silu_scaled, f_hi, f_lo = (
            sem(n) for n in ("conv_out", "silu_done", "silu_scaled", "f_hi", "f_lo"))
        y_t, y_sums, y_var, y_pow, y_rstd = (sem(n) for n in ("y_t", "y_sums", "y_var", "y_pow", "y_rstd"))
        y_columns = sem("y_columns")
        y_ready = [sem("y_ready_act"), sem("y_ready_dve")]
        ng_in, ss_clear = sem("ng_in"), sem("ss_clear")
        state_t, state_out = sem("state_t"), sem("state_out")
        y_out = sem("y_out")
        states_out = sem("states_out")

        w_in = ins["w_in"][0].rearrange("(k p) n -> p k n", p=P)
        w_a = ins["w_a_out"][0].rearrange("(k p) n -> p k n", p=P)
        w_b = ins["w_swa_o"][0].rearrange("(g j d) n -> g d j n", g=NKV, d=HD)
        w_c = ins["w_dsa_o"][0].rearrange("(g j d) n -> g d j n", g=NKV, d=HD)
        w_o = ins["w_out"][0].rearrange("(k p) n -> p k n", p=P)
        w_g = ins["w_gate"][0].rearrange("(k p) n -> p k n", p=P)
        w_u = ins["w_up"][0].rearrange("(k p) n -> p k n", p=P)
        w_d = ins["w_down"][0].rearrange("(k p) n -> p k n", p=P)

        def tile_rows(a):
            return a.rearrange("r (t p) -> (r t) p", p=P)

        def x_rows(i):
            return ins["x_prompt"][0, i * P:(i + 1) * P, :] if i < NT else ins["x_sample"][0]

        def group(k, rows=P):
            return PS[0:rows, NB * k:NB * k + NB, 0:PIECE]

        def tokens(ap):
            return ap.rearrange("p (b n) -> p b n", b=NB)

        def tile_at(buf, j):
            return buf[:, bass.ds(j, 1), :].rearrange("p a (b n) -> p (a b) n", b=NB)

        def pairs(kind, first):
            x, q, o = first
            out = []
            for i in [NT] + list(range(NT)):
                sample = i == NT
                window = kind == "window"
                for g in range(1 if sample else NKV):
                    for half in range(1 if sample else 2):
                        if sample:
                            n, first_block, blocks = PAST + DEC, 0, 2
                            mask = None if window else MASK_S[:, :]
                            sinks, negative = SINK_S[:, :], NEG_SINK[:, NH:NH + NKV]
                        else:
                            first_block = max(i - 1, 0) if window else 0
                            blocks = i + 1 - first_block
                            n = blocks * P
                            if window and i > 0:
                                mask = MASKW[:, :]
                            elif n <= TOPK:
                                mask = MASK0[:, 2 * P - n:2 * P]
                            else:
                                mask = MASK[:, SEL_AT[i]:SEL_AT[i] + n]
                            head = g * NJ + 2 * half
                            sinks, negative = SINK[:, head:head + 2], NEG_SINK[:, head:head + 2]
                        size = 1 if sample else 2
                        chunks = [list(range(a, min(a + size, blocks))) for a in range(0, blocks, size)]
                        out.append(dict(x=x, i=i, g=g, half=half, sample=sample, window=window, n=n,
                                        first=first_block, chunks=chunks, q=q, mask=mask, sinks=sinks, negative=negative, ub=x % 3,
                                        o=o, last=sample or half == 1))
                        x += 1
                        q += len(chunks)
                        o += sample or half == 1
            return out, (x, q, o)

        WINDOW, _next = pairs("window", (0, 0, 0))
        SPARSE, _next = pairs("sparse", _next)
        for kind in (WINDOW, SPARSE):
            for r, pair in enumerate(kind):
                if pair["window"]:
                    pair["at"], pair["ahead"] = (0, 12288 // 4, 14336 // 4)[r % 3], 2
                elif pair["sample"] or pair["i"] < 5:
                    pair["at"], pair["ahead"] = 5120 // 4 * (r % 3), 2
                else:
                    pair["at"], pair["ahead"] = 8192 // 4 * ((r + 1) % 2), 1
                former = kind[max(r - (3 if pair["ahead"] == 2 else 2), 0)]
                pair["free"] = former["q"] + len(former["chunks"]) if r >= 3 else 0

        def front(ps, y):
            found = [p for z, p in enumerate(ps) if z - p["ahead"] == y]
            return found[0] if found else None

        def probs_of(pair, h):
            a = pair["at"] + h * pair["n"]
            return PR[:, a:a + pair["n"]]

        def scores_of(pair, h):
            return PS[:, 2 * h:2 * h + 2, :].rearrange("p b n -> p (b n)")[:, 0:pair["n"]]

        def attn_sums(pair, g):
            rows, n = slice(HD * g, HD * (g + 1)), DEC if pair["sample"] else P
            at = pair["i"] * P
            return (PS[rows, 6 + g, 0:NJ * n].rearrange("p (j t) -> p j t", j=NJ),
                    O_HI[rows, :, at:at + n], O_LO[rows, :, at:at + n])

        def groups_of(pair):
            return range(NKV) if pair["sample"] else [pair["g"]]

        X_BATCHES = [(0, 2), (2, 4), (4, 6), (6, NT + 1)]
        R_IDX_C, R_IDX_W, R_IDX_K = 0, 1, 2
        R_B_C, R_B_V = 5, 7
        R_C_C, R_C_V = 10, 14
        TRIPLES = [(0, 4), (4, 8), (8, 9)]
        K_LAST = [(NT - 1, NT + 1)]

        block = ctx.enter_context(nc.Block())

        @block.sync
        def _(sp):
            for i in range(NT + 1):
                sp.dma_start(XIN[0:rows_of(i), i, :], x_rows(i)).then_inc(x_in[i], 16)
                if i == 1:
                    sp.dma_start(NG[:, :], ins["norm_mix"].broadcast_to([P, D])).then_inc(ng_in, 16)
                if i == 2:
                    sp.dma_start(RAW[:, 0, 0:4, :], w_in[:, 0:4, C_QI:C_QI + P]).then_inc(raw_full[0], 16)
                    sp.dma_start(RAW[:, 0, 4:8, :], w_in[:, 4:8, C_QI:C_QI + P]).then_inc(raw_full[0], 16)

            def small(dst, src, s):
                sp.dma_start(dst, src).then_inc(s, 16)

            small(V_IN[V_NORM:V_NORM + KT, :], tile_rows(ins["norm_ffn"]), misc_in)
            small(V_IN[V_CA:V_CA + 3 * CT, :], tile_rows(ins["conv_a"][0]), misc_in)
            small(V_IN[V_CF:V_CF + 3 * FT, :], tile_rows(ins["conv_ffn"][0]), misc_in)
            small(V_IN[V_NF:V_NF + KT, :], ins["norm_final"].rearrange("(t p) -> t p", p=P), misc_in)
            small(S_IN[S_CA:S_CA + 2 * CT, :], tile_rows(ins["state_conv_a"][0, 0]), misc_in)
            small(S_IN[S_CF:S_CF + 2 * FT, :], tile_rows(ins["state_ffn_conv"][0, 0]), misc_in)
            small(SINK[:, :], ins["attn_sinks"].broadcast_to([P, NH]), misc_in)

            def free(n0, i, k):
                sp.wait_ge(lo_ready, n0 + 2 * i + k - 1)
                apart(sp)

            def load(k, dst_src):
                for dst, src in dst_src:
                    sp.dma_start(dst, src).then_inc(raw_full[k], 16)

            def plain(k, src, tiles=KT):
                half = tiles // 2
                return [(RAW[:, k, 0:half, :], src[:, 0:half]), (RAW[:, k, half:tiles, :], src[:, half:tiles])]

            def columns(w, at, width=P):
                return w[:, :, at:at + width]

            load(1, plain(1, columns(w_in, C_QI + P)))
            free(J_IDX, 1, 0)
            load(0, [(RAW[:, 0, :, a * HD:(a + 1) * HD], columns(w_in, C_KI, HD)) for a in range(2)])
            free(J_IDX, 1, 1)
            load(1, [(RAW[:, 1, 0:4, 0:IDXH], w_in[:, 0:4, C_WI:C_WI + IDXH]),
                     (RAW[:, 1, 4:8, 0:IDXH], w_in[:, 4:8, C_WI:C_WI + IDXH])])
            with sp.Fori(0, CT // 2) as i:
                for m in range(6):
                    t, at = m // 3, (C_AB, C_AC, C_AX)[m % 3]
                    free(J_A + 2 * (m // 2), 3 * i, m % 2)
                    load(m % 2, plain(m % 2, w_in[:, :, bass.ds(i * (2 * P) + (at + t * P), P)]))

            def gate_loads(n0, gate, split):
                with sp.Fori(0, KT) as j:
                    free(n0, j, 0)
                    load(0, plain(0, w_in[:, :, bass.ds(j * P + (C_G + gate * D), P)]))
                    free(n0, j, 1)
                    load(1, split(j))

            def head_rows(w):
                return lambda j: [(RAW[HD * g:HD * (g + 1), 1, 0:NJ, :], w[g, :, :, bass.ds(j * P, P)])
                                  for g in range(NKV)]

            def attention_loads(n0, q, kv):
                for k in range(2):
                    free(n0, 0, k)
                    load(k, plain(k, columns(w_in, kv[k])))
                with sp.Fori(0, NJ // 2) as i:
                    for k in range(2):
                        free(n0 + 2, i, k)
                        load(k, [(RAW[:, k, :, g * HD:(g + 1) * HD],
                                  w_in[:, :, bass.ds(i * (2 * HD) + (q + k * HD + g * NJ * HD), HD)])
                                 for g in range(NKV)])

            gate_loads(J_GA, 0, lambda j: plain(1, w_a[:, :, bass.ds(j * P, P)], CT))
            attention_loads(J_B, C_QB, (C_KB, C_VB))
            gate_loads(J_GB, 1, head_rows(w_b))
            attention_loads(J_C, C_QC, (C_KC, C_VC))
            gate_loads(J_GC, 2, head_rows(w_c))
            free(J_WO, 0, 0)
            load(0, plain(0, columns(w_o, 0)))
            free(J_WO, 0, 1)
            load(1, plain(1, columns(w_o, P)))
            sp.wait_ge(job_done, J_WO)
            for i in range(0, NT, 2):
                src = ins["x_prompt"][0, i * P:(i + 2) * P, :].rearrange("(t p) d -> p t d", p=P)
                sp.dma_start(XR[:, i:i + 2, :], src).then_inc(xr_in[i // 2], 16)
            sp.dma_start(XR[0:DEC, NT, :], x_rows(NT)).then_inc(xr_in[NT // 2], 16)
            with sp.Fori(1, KT // 2) as i:
                for k in range(2):
                    free(J_WO, i, k)
                    load(k, plain(k, w_o[:, :, bass.ds(i * (2 * P) + k * P, P)]))
            f0 = 0
            for g, nf in enumerate(FFN_GROUPS):
                with sp.Fori(0, nf) as f:
                    free(J_FFN[g], f, 0)
                    load(0, plain(0, w_g[:, :, bass.ds(f * P + f0 * P, P)]))
                    free(J_FFN[g], f, 1)
                    load(1, plain(1, w_u[:, :, bass.ds(f * P + f0 * P, P)]))
                with sp.Fori(0, KT // 2) as i:
                    for k in range(2):
                        free(J_DOWN[g], i, k)
                        load(k, plain(k, w_d[:, f0:f0 + nf, bass.ds(i * (2 * P) + k * P, P)], nf))
                f0 += nf
            for i in range(NT + 1):
                sp.wait_ge(y_ready[i % 2], i // 2 + 1)
                out = outs[0][0, i * P:(i + 1) * P, :] if i < NT else outs[1][0]
                sp.dma_start(out, Y[0:rows_of(i), i, :]).then_inc(y_out, 16)
            sp.wait_ge(y_out, 16 * (NT + 1))

        @block.gpsimd
        def _(pool):
            step = Steps(pool, pool_step)

            def load(dst, src, s):
                pool.dma_start(dst, src).then_inc(s, 16)

            step.mark(nc.gpsimd.memset(IDENT[:, :], 0.0))
            step.wait()
            nc.gpsimd.affine_select(out=IDENT[:, :], in_=IDENT[:, :], compare_op=ALU.not_equal, fill=1.0,
                                    base=0, pattern=[[-1, P]], channel_multiplier=1).then_inc(const_ready, 1)
            nc.gpsimd.memset(ONES[:, :], 1.0).then_inc(const_ready, 1)

            def power(src, dst, ready, done, n):
                pool.wait_ge(ready, n)
                nc.gpsimd.tensor_tensor(dst, src[0], src[1], ALU.pow).then_inc(done, 1)

            def half(rows):
                return ss[0:rows, 3, 0:1]

            for m, (a, b) in enumerate(X_BATCHES):
                power((ss[:, 1, a:b], half(P).broadcast_to([P, b - a])), ss[:, 2, a:b], x_var, x_pow, m + 1)
            for a in range(2):
                load(KCI[:, a * HD:(a + 1) * HD], ins["cache_idx_k"][0, 0], side_in[0])

            pool.wait_ge(rows_out, R_IDX_K + 3)
            out = outs[7][0, 0].rearrange("(t p) d -> p t d", p=P)
            pool.dma_start(out, KI_ROWS[:, 0:NT, :]).then_inc(stored[0], 16)
            pool.dma_start(outs[14][0, 0], KI_ROWS[0:DEC, NT, :]).then_inc(stored[0], 16)

            def kv(d):
                return d.rearrange("t g d -> t (g d)")

            pool.wait_ge(job_done, J_B)
            pool.wait_ge(a_lo, CT + 1)
            load(KC[:, :], kv(ins["cache_swa_k"][0, 0]), side_in[1])
            load(VC[:, :], kv(ins["cache_swa_v"][0, 0]), side_in[1])
            pool.wait_ge(side_in[1], 32)
            for src, o_s in ((KC, 10), (VC, 11)):
                pool.dma_start(kv(outs[o_s][0, 0])[0:P - DEC, :], src[DEC:P, :]).then_inc(stored[1], 16)
            pool.wait_ge(rows_out, R_B_V + 3)
            for new, o_p, o_s in ((K_ROWS, 3, 10), (V_ROWS, 4, 11)):
                pool.dma_start(kv(outs[o_p][0, 0]), new[:, NT - 1, :]).then_inc(stored[1], 16)
                pool.dma_start(kv(outs[o_s][0, 0])[P - DEC:P, :], new[0:DEC, NT, :]).then_inc(stored[1], 16)

            pool.wait_ge(job_done, J_GB + 2)
            pool.wait_ge(stored[1], 16 * 6)
            load(KC[:, :], kv(ins["cache_dsa_k"][0, 0]), side_in[2])
            load(VC[:, :], kv(ins["cache_dsa_v"][0, 0]), side_in[2])
            pool.wait_ge(rows_out, R_C_V + 3)
            for new, o_p, o_s in ((K_ROWS, 5, 12), (V_ROWS, 6, 13)):
                out = kv(outs[o_p][0, 0]).rearrange("(t p) d -> p t d", p=P)
                pool.dma_start(out, new[:, 0:NT, :]).then_inc(stored[2], 16)
                pool.dma_start(kv(outs[o_s][0, 0]), new[0:DEC, NT, :]).then_inc(stored[2], 16)

            pool.wait_ge(ss_var, 1)
            nc.gpsimd.tensor_tensor(ss[0:96, 2, 0:11], ss[0:96, 1, 0:11],
                                    ss[0:96, 3, 0:1].broadcast_to([96, 11]), ALU.pow).then_inc(ss_pow, 1)
            pool.wait_ge(rb_ready, 3)
            at = 0
            for g, nf in enumerate(FFN_GROUPS):
                with pool.Fori(0, nf) as f:
                    pool.wait_ge(silu_done, f + (at + 1))
                    nc.gpsimd.tensor_tensor(T0[:, 0:TOK], T0[:, 0:TOK], T3[:, 0:TOK],
                                            ALU.mult).then_inc(silu_scaled, 1)
                at += nf
            power((ss[:, 1, 0:NT + 1], half(P).broadcast_to([P, NT + 1])), ss[:, 2, 0:NT + 1], y_var, y_pow, 1)
            pool.wait_ge(state_out, 1)
            rows = U[0:N_COLS, 0:P]
            for at, width, o_p, o_s in ((N_CA, CT, 2, 9), (N_CF, FT, 8, 15)):
                for s, o in ((0, o_p), (1, o_s)):
                    a = at + 2 * s * width
                    pool.dma_start(tile_rows(outs[o][0, 0]), rows[a:a + 2 * width, :]).then_inc(states_out, 16)
            pool.wait_ge(stored[0], 32)
            pool.wait_ge(stored[1], 16 * 6)
            pool.wait_ge(stored[2], 16 * 4)
            pool.wait_ge(states_out, 16 * 4)

        @block.tensor
        def _(pe):
            def project(n0, i, k, hi, lo, tiles=KT, rows=P, ready=None, between=None):
                pe.wait_ge(lo_ready, n0 + 2 * i + k + 1)
                if not (isinstance(i, int) and n0 + 2 * i == 0):
                    pe.wait_ge(taken[k], n0 // 2 + i)
                for t in range(tiles):
                    if ready:
                        pe.wait_ge(ready[0], ready[1] + t + 1)
                    for w, x in ((WHI, hi), (WHI, lo), (WLO, hi)):
                        for b in range(NB):
                            last = nc.tensor.matmul(
                                PS[0:rows, NB * k + b, 0:PIECE], w[:, k, t, 0:rows],
                                x[:, t, b * PIECE:(b + 1) * PIECE],
                                start=t == 0 and w is WHI and x is hi,
                                stop=t == tiles - 1 and w is WLO)
                    if t == tiles - 1:
                        last.then_inc(job_done, 1)
                    if between and t in between:
                        between[t]()

            def transpose(out, in_, s=None):
                r = in_.shape[0]
                p0 = in_.start_partition()
                last = nc.tensor.transpose(out, in_, IDENT[p0:p0 + r, p0:p0 + r])
                if s is not None:
                    last.then_inc(s, 1)

            pe.wait_ge(const_ready, 2)
            for i in range(NT + 1):
                r = rows_of(i)
                pe.wait_ge(h_rows, i + 1)
                if i >= 3:
                    pe.wait_ge(h_lo, i - 2)
                for j in range(KT):
                    transpose(PS[:, 2 * (i % 3) + j // 4, (j % 4) * P:(j % 4) * P + r],
                              HN[0:r, i % 3, j * P:(j + 1) * P], h_t if j == KT - 1 else None)
            pe.wait_ge(misc_in, 16 * 7)
            transpose(PS[:, 6, 0:VEC_ROWS], V_IN[0:VEC_ROWS, :])
            transpose(PS[:, 6, P:P + S_ROWS], S_IN[0:S_ROWS, :], tables_t)
            pe.wait_ge(h_lo, NT + 1)

            for i in range(2):
                for k in range(2):
                    rows = IDXH if (i, k) == (1, 1) else P
                    project(J_IDX, i, k, H_HI, H_LO, rows=rows)
            pe.wait_ge(side_in[0], 32)
            pe.wait_ge(tables_ready, 1)
            transpose(PS[:, 6, 0:P], KCI[:, :], rows_t)
            pe.wait_ge(taken[1], 2)
            pe.wait_ge(staged, 1)
            for i in SEL:
                transpose(PS[:, 7, IDXH * i:IDXH * (i + 1)], WIT[:, i * P:(i + 1) * P])
            transpose(PS[:, 7, IDXH * NT:IDXH * (NT + 1)], WS[:, :], rows_t)
            pe.wait_ge(taken[0], 2)
            for m, (a, b) in enumerate(TRIPLES):
                pe.wait_ge(rows_out, R_IDX_K + m - 1)
                for i in range(a, b):
                    r = rows_of(i)
                    transpose(PS[0:r, 6 + m % 2, (i - a) * HD:(i - a + 1) * HD],
                              KI[0:HD, i * P:i * P + r], rows_t if i == b - 1 else None)
            c = 0
            pe.wait_ge(taken[1], 2)
            for i in SEL + [NT]:
                n = (i + 1) * P if i < NT else PAST + DEC
                if i == NT:
                    pe.wait_ge(staged, 3)
                for h in range(IDXH):
                    p0 = HD * (h % 2)
                    if c >= 2:
                        pe.wait_ge(idx_relu, c - 1)
                    for a in range(0, n, BANK):
                        b = min(a + BANK, n)
                        out = PS[:, 2 * (c % 2) + a // BANK, 0:b - a]
                        if i == NT:
                            last = nc.tensor.matmul(out, QS2[p0:p0 + HD, h // 2, :], KSI[p0:p0 + HD, a:b],
                                                    start=True, stop=True)
                            continue
                        q = slice(i * P, (i + 1) * P)
                        nc.tensor.matmul(out, QI[:, h, q], KI_HI[:, a:b], start=True, stop=False)
                        last = nc.tensor.matmul(out, QI[p0:p0 + HD, h, q], KI_LO[p0:p0 + HD, a:b],
                                                start=False, stop=True)
                    last.then_inc(idx_s, 1)
                    c += 1
            pe.wait_ge(idx_relu, c)

            with pe.Fori(0, CT // 2) as i:
                for m in range(6):
                    project(J_A + 2 * (m // 2), 3 * i, m % 2, H_HI, H_LO)
            def gates(n0, hi, lo, ready, count):
                with pe.Fori(0, KT) as j:
                    project(n0, j, 0, H_HI, H_LO)
                    pe.wait_ge(ready, count)
                    project(n0, j, 1, hi, lo, tiles=CT)

            gates(J_GA, A_HI, A_LO, a_lo, CT + 1)

            def row_group(r, src, a, b):
                pe.wait_ge(rows_out, r - 1)
                for i in range(a, b):
                    n = rows_of(i)
                    transpose(PS[0:n, 6 + r % 2, (i - a) * P:(i - a + 1) * P],
                              src[:, i * P:i * P + n], rows_t if i == b - 1 else None)

            def attention_jobs(n0, side, r_c, k_tiles):
                def cached():
                    pe.wait_ge(side_in[side], 32)
                    pe.wait_ge(rows_out, r_c)
                    transpose(PS[:, 6 + r_c % 2, 0:P], KC[:, :], rows_t)

                def group_of(r, src, a, b):
                    return lambda: row_group(r, src, a, b)

                for k in range(2):
                    project(n0, 0, k, H_HI, H_LO)
                pe.wait_ge(taken[0], n0 // 2 + 1)
                keys = [group_of(r_c + 1 + m, K_T, a, b) for m, (a, b) in enumerate(k_tiles)]
                r_v = r_c + 1 + len(keys)
                project(n0, 1, 0, H_HI, H_LO, between={1: cached, **{3 + 2 * m: g for m, g in enumerate(keys)}})
                pe.wait_ge(taken[1], n0 // 2 + 1)
                project(n0, 1, 1, H_HI, H_LO)
                values = [group_of(r_v + m, V_T, a, b) for m, (a, b) in enumerate(TRIPLES)]
                project(n0, 2, 0, H_HI, H_LO, between=dict(zip((0, 1, 5), values)))
                project(n0, 2, 1, H_HI, H_LO)
                for k in range(2):
                    pe.wait_ge(taken[k], n0 // 2 + 3)
                pe.wait_ge(rows_out, r_v + 3)

            def qk(pair, h):
                x, n = pair["x"], pair["n"]
                if x > 0:
                    pe.wait_ge(masked, 2 * (x - 1) + h + 1)
                if pair["sample"]:
                    pe.wait_ge(staged, 5 if pair["window"] else 7)
                    rows = slice(HD * h, HD * (h + 1))
                    last = nc.tensor.matmul(PS[:, 2 * h, 0:n], QS[rows, :], KS[rows, :], start=True, stop=True)
                else:
                    rows = slice(HD * pair["g"], HD * (pair["g"] + 1))
                    j, at = 2 * pair["half"] + h, pair["i"] * P
                    for a in range(0, n, BANK):
                        b = min(a + BANK, n)
                        k0 = pair["first"] * P
                        for q, k in ((Q_HI, K_HI), (Q_HI, K_LO), (Q_LO, K_HI)):
                            last = nc.tensor.matmul(PS[:, 2 * h + a // BANK, 0:b - a], q[rows, j, at:at + P],
                                                    k[rows, k0 + a:k0 + b], start=q is Q_HI and k is K_HI,
                                                    stop=q is Q_LO)
                last.then_inc(s_done, 1)

            def pt(pair, c):
                q = pair["q"] + c
                for h in range(2):
                    pe.wait_ge(probs[h], pair["x"] + 1)
                if q >= 2:
                    pe.wait_ge(pt_hi, q - 1)
                    pe.wait_ge(pt_lo, q - 1)
                for at, b in enumerate(pair["chunks"][c]):
                    rows = DEC if pair["sample"] and b == 1 else P
                    for h in range(2):
                        last = h == 1 and b == pair["chunks"][c][-1]
                        transpose(PS[0:rows, 4 + q % 2, (2 * at + h) * P:(2 * at + h + 1) * P],
                                  probs_of(pair, h)[:, b * P:b * P + rows], pt_done if last else None)

            def pv(pair, c):
                q, g = pair["q"] + c, pair["g"]
                pe.wait_ge(pt_hi, q + 1)
                pe.wait_ge(pt_lo, q + 1)
                if c == 0 and pair["half"] == 0:
                    before = pair["o"] - (1 if pair["sample"] or (pair["i"], g) == (0, 0) else 2)
                    if before >= 0:
                        pe.wait_ge(o_lo, before + 1)
                blocks = len(pair["chunks"]) * (1 if pair["sample"] else 2)
                for at, b in enumerate(pair["chunks"][c]):
                    if pair["sample"]:
                        v, rows = (VC[:, :], P) if b == 0 else (VS[0:DEC, :], DEC)
                        for h in range(NKV):
                            last = nc.tensor.matmul(PS[:, 6 + h, 0:P], v, PT_S[0:rows, q % 2, h * P:(h + 1) * P],
                                                    start=b == 0, stop=b == 1)
                        continue
                    key = pair["first"] + b
                    end = b == pair["chunks"][-1][-1]
                    for v, p in ((V_HI, PT_HI), (V_HI, PT_LO), (V_LO, PT_HI)):
                        last = nc.tensor.matmul(PS[:, 6 + g, 2 * P * pair["half"]:2 * P * (pair["half"] + 1)],
                                                v[:, key, :], p[:, q % 2, 2 * P * at:2 * P * (at + 1)],
                                                start=b == 0 and v is V_HI and p is PT_HI,
                                                stop=end and v is V_LO)
                last.then_inc(pv_done, 1)

            def attend(ps):
                for pair in ps[0:2]:
                    qk(pair, 0)
                    qk(pair, 1)
                for y, pair in enumerate(ps):
                    late = y + 2 < len(ps) and ps[y + 2]["ahead"] == 1
                    if y + 2 < len(ps) and not late:
                        qk(ps[y + 2], 0)
                        qk(ps[y + 2], 1)
                    pt(pair, 0)
                    if y > 0:
                        pv(ps[y - 1], len(ps[y - 1]["chunks"]) - 1)
                    for c in range(1, len(pair["chunks"])):
                        pt(pair, c)
                        pv(pair, c - 1)
                    if late:
                        qk(ps[y + 2], 0)
                        qk(ps[y + 2], 1)
                last = ps[-1]
                pv(last, len(last["chunks"]) - 1)
                pe.wait_ge(masked, 2 * (last["x"] + 1))

            attention_jobs(J_B, 1, R_B_C, K_LAST)
            attend(WINDOW)
            gates(J_GB, O_HI, O_LO, o_lo, WINDOW[-1]["o"] + 1)
            attention_jobs(J_C, 2, R_C_C, TRIPLES)
            attend(SPARSE)
            gates(J_GC, O_HI, O_LO, o_lo, SPARSE[-1]["o"] + 1)

            def x_tile(i):
                def run():
                    pe.wait_ge(xr_in[i // 2], 16)
                    pe.wait_ge(xr_out, i)
                    r = rows_of(i)
                    for j in range(KT):
                        transpose(PS[:, 6 + j // 4, (j % 4) * P:(j % 4) * P + r],
                                  XR[0:r, i, j * P:(j + 1) * P], xr_t if j == KT - 1 else None)
                return run

            project(J_WO, 0, 0, M_HI, M_LO, ready=(m_lo, 0), between={t: x_tile(t - 5) for t in (5, 6, 7)})
            project(J_WO, 0, 1, M_HI, M_LO, between={t: x_tile(t + 3) for t in range(6)})
            with pe.Fori(1, KT // 2) as i:
                for k in range(2):
                    project(J_WO, i, k, M_HI, M_LO)

            for g, nf in enumerate(FFN_GROUPS):
                first = 0
                if g == 0:
                    first = 1
                    def square_sums():
                        pe.wait_ge(ssq_sum, KT + 1)
                        for i in range(11):
                            last = nc.tensor.matmul(PS[0:96, 6, i:i + 1], T0[:, i * 96:(i + 1) * 96],
                                                    ONES[:, :], start=True, stop=True)
                        last.then_inc(ss_done, 1)

                    def scales(m):
                        pe.wait_ge(ss_rstd, 1)
                        if m == 2:
                            pe.wait_ge(rb_ready, 1)
                        for i in range(5 * m, min(5 * m + 5, 11)):
                            last = nc.tensor.matmul(PS[:, 7 - m % 2, (i - 5 * m) * 96:(i - 5 * m + 1) * 96],
                                                    ss[0:96, 2, i:i + 1].broadcast_to([96, P]),
                                                    IDENT[0:96, 0:96], start=True, stop=True)
                        last.then_inc(rb_done, 1)

                    project(J_FFN[0], 0, 0, G_HI, G_LO, ready=(g_lo, 0), between={KT - 1: square_sums})
                    project(J_FFN[0], 0, 1, G_HI, G_LO,
                            between={m + 3: lambda m=m: scales(m) for m in range(3)})
                with pe.Fori(first, nf) as f:
                    project(J_FFN[g], f, 0, G_HI, G_LO)
                    project(J_FFN[g], f, 1, G_HI, G_LO)
                with pe.Fori(0, KT // 2) as i:
                    for k in range(2):
                        project(J_DOWN[g], i, k, F_HI, F_LO, tiles=nf, ready=(f_lo, sum(FFN_GROUPS[:g])))
            pe.wait_ge(rb_ready, 3)
            transpose(PS[0:N_COLS, 6, 0:P], NEW[:, :], state_t)
            pe.wait_ge(ssq_sum, 2 * KT + 2)
            for i in range(NT + 1):
                r = rows_of(i)
                last = nc.tensor.matmul(PS[0:r, 7, i:i + 1], T0[:, i * P:i * P + r], ONES[:, :],
                                        start=True, stop=True)
            last.then_inc(y_sums, 1)
            pe.wait_ge(y_columns, KT)
            for k in range(2):
                pe.wait_ge(taken[k], J_END // 2)
            for i in range(NT + 1):
                r = rows_of(i)
                if i >= 3:
                    pe.wait_ge(y_ready[(i - 3) % 2], (i - 3) // 2 + 1)
                for j in range(KT):
                    transpose(PS[0:r, 2 * (i % 3) + j // 4, (j % 4) * P:(j % 4 + 1) * P],
                              XG[:, j, i * P:i * P + r], y_t if j == KT - 1 else None)

        @block.scalar
        def _(act):
            def copy(out, in_):
                return nc.scalar.activation(out, in_, ACT.Copy)

            def split(n0, i, k):
                act.wait_ge(raw_full[k], 32 * (n0 // 2 + i + 1))
                if not (isinstance(i, int) and n0 + 2 * i == 0):
                    act.wait_ge(job_done, n0 + 2 * i + k - 1)
                copy(WHI[:, k, :, :], RAW[:, k, :, :]).then_inc(hi_ready, 1)

            def following(n0, i, k):
                split(n0, i, 1) if k == 0 else split(n0, i + 1, 0)

            def done(n0, i, k):
                act.wait_ge(job_done, n0 + 2 * i + k + 1)

            def h_high(i):
                r = rows_of(i)
                act.wait_ge(h_t, i + 1)
                src = PS[:, 2 * (i % 3):2 * (i % 3) + 2, :].rearrange("p b (j t) -> p (b j) t", t=P)
                copy(H_HI[:, :, i * P:i * P + r], src[:, :, 0:r]).then_inc(h_hi, 1)

            for i in range(NT + 1):
                r = rows_of(i)
                act.wait_ge(x_in[i], 16)
                if i >= 1:
                    act.wait_ge(x_sq, i)
                else:
                    act.wait_ge(ss_clear, 1)
                nc.scalar.activation(XJ[0:r, :], XIN[0:r, i, :], ACT.Square,
                                     accum_out=ss[0:r, 0, i:i + 1]).then_inc(x_sq, 1)
                if i >= 5:
                    h_high(i - 5)
            for i in range(NT - 4, NT + 1):
                h_high(i)
            act.wait_ge(tables_t, 1)
            copy(VEC[:, 0:VEC_ROWS], PS[:, 6, 0:VEC_ROWS])
            copy(VEC[:, VEC_ROWS:VEC_ROWS + S_ROWS], PS[:, 6, P:P + S_ROWS]).then_inc(tables_ready, 1)

            split(0, 0, 0)
            for n in range(4):
                i, k = n // 2, n % 2
                following(J_IDX, i, k)
                done(J_IDX, i, k)
                if n < 2:
                    for p0 in (0, HD):
                        rows = slice(p0, p0 + HD)
                        last = nc.scalar.mul(tokens(QI[rows, 2 * n + p0 // HD, :]),
                                             PS[rows, NB * k:NB * k + NB, 0:PIECE], SCALE)
                    last.then_inc(idx_hi, 1)
                elif n == 2:
                    copy(tokens(KI[:, :]), group(k))
                    copy(tokens(KI_HI[:, :]), group(k)).then_inc(idx_hi, 1)
                else:
                    nc.scalar.mul(tokens(WIT[:, :]), group(k, IDXH), IDXH ** -0.5).then_inc(taken[k], 1)
            act.wait_ge(rows_t, R_IDX_C + 1)
            act.wait_ge(tables_ready, 1)
            copy(KSI[:, 0:PAST], PS[:, 6, 0:PAST]).then_inc(rows_out, 1)
            act.wait_ge(rows_t, R_IDX_W + 1)
            w0 = IDXH * SEL[0]
            copy(WI[:, w0:IDXH * (NT + 1)], PS[:, 7, w0:IDXH * (NT + 1)]).then_inc(rows_out, 1)
            for m, (a, b) in enumerate(TRIPLES):
                act.wait_ge(rows_t, R_IDX_K + m + 1)
                r = rows_of(a)
                copy(KI_ROWS[0:r, a:b, :], PS[0:r, 6 + m % 2, 0:(b - a) * HD].rearrange("p (t d) -> p t d", d=HD)
                     ).then_inc(rows_out, 1)
            c = 0
            for i in SEL + [NT]:
                n = (i + 1) * P if i < NT else PAST + DEC
                for h in range(IDXH):
                    act.wait_ge(idx_s, c + 1)
                    if c >= 2:
                        act.wait_ge(idx_sum, c - 1)
                    src = PS[:, 2 * (c % 2):2 * (c % 2) + 2, :].rearrange("p b n -> p (b n)")[:, 0:n]
                    nc.scalar.activation(S_SB[:, c % 2, 0:n], src, ACT.Relu).then_inc(idx_relu, 1)
                    c += 1

            with act.Fori(0, CT // 2) as i:
                for m in range(6):
                    n0, k, t = J_A + 2 * (m // 2), m % 2, m // 3
                    following(n0, 3 * i, k)
                    done(n0, 3 * i, k)
                    if m % 3 == 0:
                        act.wait_ge(a_lo, 2 * i + t + 1)
                        copy(tokens(T0[:, 0:TOK]), group(k)).then_inc(taken[k], 1)
                    elif m % 3 == 1:
                        copy(tokens(T1[:, 0:TOK]), group(k)).then_inc(taken[k], 1)
                    else:
                        act.wait_ge(a_sum, 2 * i + t + 1)
                        apart(act)
                        copy(tile_at(A_HI, 2 * i + t), tokens(T1[:, 0:TOK])).then_inc(a_hi, 1)

            def gates(n0, merged=False):
                with act.Fori(0, KT) as j:
                    following(n0, j, 0)
                    done(n0, j, 0)
                    act.wait_ge(taken[1], n0 // 2 + j)
                    nc.scalar.activation(tokens(T0[:, 0:TOK]), group(0), ACT.Sigmoid).then_inc(taken[0], 1)
                    following(n0, j, 1)
                    if merged:
                        act.wait_ge(sum_ready, j + 1)
                        apart(act)
                        copy(tile_at(M_HI, j), tokens(T3[:, 0:TOK])).then_inc(m_hi, 1)

            gates(J_GA)

            def attention_jobs(n0, side, r_c, k_tiles):
                following(n0, 0, 0)
                done(n0, 0, 0)
                if n0 == J_B:
                    act.wait_ge(stored[0], 32)
                copy(tokens(K_T[:, :]), group(0))
                copy(tokens(K_HI[:, :]), group(0)).then_inc(q_hi, 1)
                following(n0, 0, 1)
                done(n0, 0, 1)
                copy(tokens(V_T[:, :]), group(1)).then_inc(taken[1], 1)
                for m in range(NJ):
                    i, k = 1 + m // 2, m % 2
                    following(n0, i, k)
                    if m == 0:
                        act.wait_ge(rows_t, r_c + 1)
                        copy(KS[:, 0:PAST], PS[:, 6 + r_c % 2, 0:PAST]).then_inc(rows_out, 1)
                        rows_from(K_ROWS, k_tiles, r_c + 1, side)
                    if m == 2:
                        act.wait_ge(staged, 4 if side == 1 else 6)
                        rows_from(V_ROWS, TRIPLES, r_c + 1 + len(k_tiles), side)
                    done(n0, i, k)
                    copy(tokens(Q_HI[:, m, :]), group(k)).then_inc(q_hi, 1)

            def rows_from(dst, tiles, r, side):
                for m, (a, b) in enumerate(tiles):
                    act.wait_ge(rows_t, r + m + 1)
                    bank = 6 + (r + m) % 2
                    if b - a == 2:
                        copy(dst[:, a, :], PS[:, bank, 0:P])
                        copy(dst[0:DEC, a + 1, :], PS[0:DEC, bank, P:2 * P]).then_inc(rows_out, 1)
                        continue
                    n = rows_of(a)
                    src = PS[0:n, bank, 0:(b - a) * P].rearrange("p (t d) -> p t d", d=P)
                    if dst is V_ROWS and n == P:
                        copy(V_HI[:, a:b, :], src).then_inc(v_hi, 1)
                        act.wait_ge(v_lo, 2 * (side - 1) + m + 1)
                    elif dst is V_ROWS:
                        copy(VS[0:n, :], src[:, 0, :])
                    copy(dst[0:n, a:b, :], src).then_inc(rows_out, 1)

            def exp(pair, h):
                x, ub = pair["x"], pair["ub"]
                act.wait_ge(negated, 2 * x + (2 if pair["window"] else h + 1))
                p = probs_of(pair, h)
                nc.scalar.activation(p, p, ACT.Exp, bias=stat[:, ub, 1, h:h + 1],
                                     accum_out=stat[:, ub, 2, h:h + 1]).then_inc(exp_done, 1)
                if h == 1 and pair["window"]:
                    act.wait_ge(sink_shift, x + 1)
                    nc.scalar.activation(stat[:, ub, 4, :], stat[:, ub, 3, :], ACT.Exp).then_inc(sink_exp, 1)

            def normalise(pair, h):
                act.wait_ge(inverse, 2 * pair["x"] + h + 1)
                p = probs_of(pair, h)
                nc.scalar.activation(p, p, ACT.Copy, scale=stat[:, pair["ub"], 5, h:h + 1]).then_inc(probs[h], 1)

            def pt_high(pair, c):
                q = pair["q"] + c
                act.wait_ge(pt_done, q + 1)
                if q >= 2:
                    act.wait_ge(pv_done, q - 1)
                if pair["sample"]:
                    rows = DEC if c == 1 else P
                    copy(PT_S[0:rows, q % 2, 0:P], PS[0:rows, 4 + q % 2, 0:P]).then_inc(pt_hi, 1)
                else:
                    n = 2 * P * len(pair["chunks"][c])
                    copy(PT_HI[:, q % 2, 0:n], PS[:, 4 + q % 2, 0:n]).then_inc(pt_hi, 1)

            def output(pair):
                act.wait_ge(pv_done, pair["q"] + len(pair["chunks"]))
                for g in groups_of(pair):
                    src, high, _ = attn_sums(pair, g)
                    last = copy(high, src)
                last.then_inc(o_hi, 1)

            def attend(ps):
                for pair in ps[0:2]:
                    exp(pair, 0)
                    exp(pair, 1)
                normalise(ps[0], 1)
                for y, pair in enumerate(ps):
                    ahead, count = front(ps, y), len(pair["chunks"])
                    after = ps[y + 1] if y + 1 < len(ps) else None
                    for c in range(max(count, 4)):
                        if c < count:
                            pt_high(pair, c)
                        if c == 0 and after and after["ahead"] == 2:
                            normalise(after, 1)
                        if c < 2 and ahead:
                            exp(ahead, c)
                        if c == 2 and after and after["ahead"] == 1:
                            normalise(after, 1)
                    if y > 0 and ps[y - 1]["last"]:
                        output(ps[y - 1])
                output(ps[-1])

            attention_jobs(J_B, 1, R_B_C, K_LAST)
            attend(WINDOW)
            act.wait_ge(stored[1], 16 * 6)
            gates(J_GB)
            attention_jobs(J_C, 2, R_C_C, TRIPLES)
            attend(SPARSE)
            act.wait_ge(stored[2], 16 * 4)
            gates(J_GC, merged=True)

            following(J_WO, 0, 0)
            for i in range(NT + 1):
                r = rows_of(i)
                act.wait_ge(xr_t, i + 1)
                src = PS[:, 6:8, :].rearrange("p b (j t) -> p (b j) t", t=P)
                copy(X2[:, :, i * P:i * P + r], src[:, :, 0:r]).then_inc(xr_out, 1)
            def residual(i, k):
                j = 2 * i + k
                act.wait_ge(taken[k], J_WO // 2 + i + 1)
                apart(act)
                nc.scalar.activation(tile_at(G_HI, j), tile_at(X2, j), ACT.Copy,
                                     scale=vec_at(j, V_NORM)).then_inc(g_hi, 1)
                act.wait_ge(ssq_sum, j + 1)
                apart(act)
                nc.scalar.activation(tokens(T1[:, 0:TOK]), tile_at(X2, j), ACT.Square).then_inc(res_sq, 1)

            following(J_WO, 0, 1)
            residual(0, 0)
            residual(0, 1)
            with act.Fori(1, KT // 2) as i:
                for k in range(2):
                    following(J_WO, i, k)
                    residual(i, k)

            def ffn(g, f, f0):
                following(J_FFN[g], f, 0)
                if isinstance(f, int):
                    following(J_FFN[g], f, 1)
                act.wait_ge(conv_out, f + (f0 + 1))
                nc.scalar.activation(T0[:, 0:SEQ], T1[:, 0:SEQ], ACT.Silu)
                nc.scalar.activation(T0[:, SEQ:TOK], T1[:, SEQ + 2:TOK + 2], ACT.Silu).then_inc(silu_done, 1)
                if not isinstance(f, int):
                    following(J_FFN[g], f, 1)
                act.wait_ge(taken[1], J_FFN[g] // 2 + f + 1)
                apart(act)
                copy(tile_at(F_HI, f), tokens(T0[:, 0:TOK])).then_inc(f_hi, 1)

            f0 = 0
            for g, nf in enumerate(FFN_GROUPS):
                if g == 0:
                    ffn(0, 0, 0)
                with act.Fori(1 if g == 0 else 0, nf) as f:
                    ffn(g, f, f0)
                last_group = g == len(FFN_GROUPS) - 1
                count = KT // 2
                if not last_group:
                    with act.Fori(0, count) as i:
                        following(J_DOWN[g], i, 0)
                        following(J_DOWN[g], i, 1)
                f0 += nf

            def final(i, k):
                j = 2 * i + k
                act.wait_ge(taken[k], J_DOWN[-1] // 2 + i + 1)
                apart(act)
                nc.scalar.activation(tile_at(XG, j), tile_at(X2, j), ACT.Copy,
                                     scale=vec_at(j, V_NF)).then_inc(y_columns, 1)
                act.wait_ge(ssq_sum, j + (KT + 2))
                apart(act)
                nc.scalar.activation(tokens(T1[:, 0:TOK]), tile_at(X2, j), ACT.Square).then_inc(res_sq, 1)

            with act.Fori(0, KT // 2 - 1) as i:
                for k in range(2):
                    following(J_DOWN[-1], i, k)
                    final(i, k)
            i = KT // 2 - 1
            following(J_DOWN[-1], i, 0)
            final(i, 0)
            final(i, 1)
            act.wait_ge(state_t, 1)
            copy(U[0:N_COLS, 0:P], PS[0:N_COLS, 6, 0:P]).then_inc(state_out, 1)
            act.wait_ge(y_rstd, 1)
            for i in range(0, NT + 1, 2):
                r = rows_of(i)
                act.wait_ge(y_t, i + 1)
                nc.scalar.activation(Y[0:r, i, :],
                                     PS[0:r, 2 * (i % 3):2 * (i % 3) + 2, :].rearrange("p b n -> p (b n)"),
                                     ACT.Copy, scale=ss[0:r, 2, i:i + 1]).then_inc(y_ready[0], 1)

        @block.vector
        def _(dve):
            step = Steps(dve, vector_step)
            V_ = nc.vector

            def split(n0, i, k):
                dve.wait_ge(hi_ready, n0 + 2 * i + k + 1)
                V_.tensor_tensor(WLO[:, k, :, :], RAW[:, k, :, :], WHI[:, k, :, :].bitcast(F32),
                                 ALU.subtract).then_inc(lo_ready, 1)

            def following(n0, i, k):
                split(n0, i, 1) if k == 0 else split(n0, i + 1, 0)

            def done(n0, i, k):
                dve.wait_ge(job_done, n0 + 2 * i + k + 1)

            def rsqrt(rows, var, power, power_done, n):
                dve.wait_ge(power_done, n)
                t = ss[0:rows, 0, 0:var.shape[1]]
                if var.shape[1] <= 3:
                    t = ss[0:rows, 3, 12 - var.shape[1]:12]
                step.mark(V_.tensor_tensor(t, power, power, ALU.mult))
                step.wait()
                step.mark(V_.tensor_tensor(t, t, var, ALU.mult))
                step.wait()
                step.mark(V_.tensor_scalar(t, t, -0.5, 1.5, ALU.mult, ALU.add))
                step.wait()
                return V_.tensor_tensor(power, power, t, ALU.mult)

            step.mark(V_.memset(SS[:, :], 1.0))
            step.wait()
            V_.memset(ss[:, 3, 0:1], -0.5).then_inc(ss_clear, 1)
            step.mark(V_.memset(MASK0[:, :], 0.0))
            step.mark(V_.memset(MASKW[:, :], 0.0))
            step.wait()
            V_.memset(MASK0[0:CHUNK, 2 * P - CHUNK:2 * P], NEG)
            V_.memset(MASKW[0:CHUNK, 2 * P - CHUNK:2 * P], NEG)
            V_.memset(MASKW[CHUNK:P, 0:CHUNK], NEG)
            def h_low(i):
                r = rows_of(i)
                dve.wait_ge(h_hi, i + 1)
                src = PS[:, 2 * (i % 3):2 * (i % 3) + 2, :].rearrange("p b (j t) -> p (b j) t", t=P)[:, :, 0:r]
                V_.tensor_tensor(H_LO[:, :, i * P:i * P + r], src,
                                 H_HI[:, :, i * P:i * P + r].bitcast(F32), ALU.subtract).then_inc(h_lo, 1)

            done_low = 0

            def x_variance(m):
                a, b = X_BATCHES[m]
                dve.wait_ge(x_sq, b)
                V_.tensor_scalar(ss[:, 1, a:b], ss[:, 0, a:b], 1.0 / D, EPS,
                                 ALU.mult, ALU.add).then_inc(x_var, 1)

            x_variance(0)
            dve.wait_ge(ng_in, 16)
            for m, (a, b) in enumerate(X_BATCHES):
                dve.wait_ge(x_var, m + 1)
                step.mark(rsqrt(P, ss[:, 1, a:b], ss[:, 2, a:b], x_pow, m + 1))
                step.wait()
                for i in range(a, b):
                    r = rows_of(i)
                    if i >= 3:
                        dve.wait_ge(h_t, i - 2)
                    V_.scalar_tensor_tensor(HN[0:r, i % 3, :], XIN[0:r, i, :], ss[0:r, 2, i:i + 1],
                                            NG[0:r, :], ALU.mult, ALU.mult).then_inc(h_rows, 1)
                    if i == a and m + 1 < len(X_BATCHES):
                        x_variance(m + 1)
                    if i >= 2:
                        h_low(i - 2)
                        done_low += 1
            for i in range(done_low, NT + 1):
                h_low(i)

            split(0, 0, 0)
            dve.wait_ge(misc_in, 16 * 7)
            for j in range(NJ):
                V_.tensor_copy(SINK_S[DEC * j:DEC * (j + 1), :], SINK[DEC * j:DEC * (j + 1), j:NH:NJ])
                V_.tensor_scalar(NEG_SINK[DEC * j:DEC * (j + 1), NH:NH + NKV],
                                 SINK[DEC * j:DEC * (j + 1), j:NH:NJ], -1.0, None, ALU.mult)
            step.mark(V_.tensor_scalar(NEG_SINK[:, 0:NH], SINK[:, :], -1.0, None, ALU.mult))
            step.wait()
            for n in range(4):
                k = n % 2
                following(J_IDX, n // 2, k)
                if n == 3:
                    continue
                dve.wait_ge(idx_hi, n + 1)
                if n == 2:
                    V_.tensor_tensor(tokens(KI_LO[:, :]), group(k), tokens(KI_HI[:, :]).bitcast(F32),
                                     ALU.subtract).then_inc(taken[k], 1)
                    continue
                for p0 in (0, HD):
                    rows, other = slice(p0, p0 + HD), slice(HD - p0, 2 * HD - p0)
                    h = 2 * n + p0 // HD
                    V_.scalar_tensor_tensor(tokens(QI[other, h, :]), PS[rows, NB * k:NB * k + NB, 0:PIECE], SCALE,
                                            tokens(QI[rows, h, :]).bitcast(F32), ALU.mult, ALU.subtract)
                at = SEQ - 2 * PIECE
                V_.tensor_scalar(QS2[:, n, :].rearrange("p (r t) -> p r t", t=DEC),
                                 PS[:, NB * k + 2, at:at + DEC].unsqueeze(1).broadcast_to([P, 4, DEC]),
                                 SCALE, None, ALU.mult).then_inc(taken[k], 1)
            dve.wait_ge(taken[1], 2)
            V_.tensor_copy(WS[:, :].rearrange("p (r t) -> p r t", t=DEC),
                           WIT[:, SEQ:TOK].unsqueeze(1).broadcast_to([IDXH, 4, DEC])).then_inc(staged, 1)
            dve.wait_ge(taken[0], 2)
            dve.wait_ge(rows_out, R_IDX_C + 1)
            V_.tensor_copy(KSI[:, PAST:PAST + DEC], KI[:, SEQ:TOK]).then_inc(staged, 2)

            def score(i):
                return MASK[:, SEL_AT[i]:SEL_AT[i] + (i + 1) * P] if i < NT else MASK_S[:, :]

            dve.wait_ge(rows_out, R_IDX_W + 1)
            c = 0
            for i in SEL + [NT]:
                s = score(i)
                n = s.shape[1]
                for h in range(IDXH):
                    w = WI[:, IDXH * i + h:IDXH * i + h + 1]
                    dve.wait_ge(idx_relu, c + 1)
                    if h == 0:
                        V_.tensor_scalar(s, S_SB[:, c % 2, 0:n], w, None, ALU.mult).then_inc(idx_sum, 1)
                    else:
                        dve.wait_ge(idx_sum, c)
                        V_.scalar_tensor_tensor(s, S_SB[:, c % 2, 0:n], w, s, ALU.mult,
                                                ALU.add).then_inc(idx_sum, 1)
                    c += 1
                if i < NT:
                    dve.wait_ge(idx_sum, c)
                    step.mark(V_.memset(s[0:CHUNK, n - CHUNK:n], NEG))
            step.wait()

            def select(*work):
                after = {}
                for r in range(max(rounds for _, rounds in work)):
                    for find in (True, False):
                        for slot, (i, rounds) in enumerate(work):
                            if r >= rounds:
                                continue
                            s, top = score(i), TOP8[:, 8 * slot:8 * slot + 8]
                            if slot in after:
                                step.wait(after[slot])
                            else:
                                step.wait()
                            apart(dve)
                            step.mark(V_.max(top, s) if find else V_.match_replace(s, top, s, TAKEN))
                            after[slot] = step.marked
                step.wait()

            def to_mask(i):
                step.mark(V_.tensor_scalar(score(i), score(i), TAKEN, NEG, ALU.not_equal, ALU.mult))
                step.wait()

            def conv_input(k, other):
                full = 2 * PIECE
                V_.tensor_tensor(U[:, 2:2 + full].rearrange("p (b n) -> p b n", b=2),
                                 PS[:, NB * k:NB * k + 2, 0:PIECE],
                                 other[:, 0:full].rearrange("p (b n) -> p b n", b=2), ALU.mult)
                V_.tensor_tensor(U[:, 2 + full:2 + SEQ], PS[:, NB * k + 2, 0:SEQ - full],
                                 other[:, full:SEQ], ALU.mult)
                V_.tensor_tensor(U[:, SEQ + 4:TOK + 4], PS[:, NB * k + 2, SEQ - full:PIECE],
                                 other[:, SEQ:TOK], ALU.mult).then_inc(taken[k], 1)

            def states(t, width, at_state, at_new):
                old = VEC[:, VEC_ROWS + at_state:VEC_ROWS + at_state + 2 * width].rearrange("p (s t) -> p s t", s=2)
                new = NEW[:, at_new:at_new + 4 * width].rearrange("p (s t) -> p s t", s=4)
                V_.tensor_copy(new[:, 0:2, bass.ds(t, 1)], U[:, SEQ:SEQ + 2].unsqueeze(2))
                V_.tensor_copy(new[:, 2:4, bass.ds(t, 1)], U[:, TOK + 2:TOK + 4].unsqueeze(2))
                step.mark(V_.tensor_copy(U[:, SEQ + 2:SEQ + 4].unsqueeze(2), old[:, :, bass.ds(t, 1)]))
                step.wait()

            def convolve(taps, out):
                n = TOK + 2
                step.mark(V_.tensor_scalar(out[:, 0:n], U[:, 0:n], taps[0], None, ALU.mult))
                for w in (1, 2):
                    step.wait()
                    last = V_.scalar_tensor_tensor(out[:, 0:n], U[:, w:n + w], taps[w], out[:, 0:n],
                                                   ALU.mult, ALU.add)
                    if w == 1:
                        step.mark(last)
                return last

            V_.memset(U[:, 0:2], 0.0).then_inc(a_lo, 1)
            dve.wait_ge(tables_ready, 1)
            ROUNDS = TOPK // 8
            with dve.Fori(0, CT // 2) as i:
                with step.loop(i, CT // 2, 2 * (1 + 3) + 2 * 4 * (ROUNDS // 8 + ROUNDS // 16)):
                    for m in range(6):
                        n0, k, t = J_A + 2 * (m // 2), m % 2, m // 3
                        following(n0, 3 * i, k)
                        if m % 3 != 2:
                            select((SEL[3], ROUNDS // 8), (SEL[0], ROUNDS // 16))
                            continue
                        done(n0, 3 * i, k)
                        dve.wait_ge(taken[1 - k], J_A // 2 + 3 * i + (m - 1) // 2 + 1)
                        conv_input(k, T1)
                        dve.wait_ge(taken[k], n0 // 2 + 3 * i + 1)
                        states(2 * i + t, CT, S_CA, N_CA)
                        step.mark(convolve([vec_at(2 * i + t, V_CA + w * CT) for w in range(3)], T3))
                        step.wait()
                        V_.tensor_tensor(T1[:, 0:SEQ], T3[:, 0:SEQ], T0[:, 0:SEQ], ALU.mult)
                        V_.tensor_tensor(T1[:, SEQ:TOK], T3[:, SEQ + 2:TOK + 2], T0[:, SEQ:TOK],
                                         ALU.mult).then_inc(a_sum, 1)
                        dve.wait_ge(a_hi, 2 * i + t + 1)
                        V_.tensor_tensor(tile_at(A_LO, 2 * i + t), tokens(T1[:, 0:TOK]),
                                         tile_at(A_HI, 2 * i + t).bitcast(F32),
                                         ALU.subtract).then_inc(a_lo, 1)

            def gates(n0, mode, before=(), later=()):
                with dve.Fori(0, KT) as j:
                    with step.loop(j, KT, 2 * sum(rounds for _, rounds in (*before, *later))):
                        following(n0, j, 0)
                        if before:
                            select(*before)
                        following(n0, j, 1)
                        if later:
                            select(*later)
                        done(n0, j, 1)
                        dve.wait_ge(taken[0], n0 // 2 + j + 1)
                        gate = tokens(T0[:, 0:TOK])
                        acc = tile_at(MACC, j)
                        if mode == "first":
                            V_.tensor_tensor(acc, group(1), gate, ALU.mult).then_inc(taken[1], 1)
                        else:
                            V_.tensor_tensor(tokens(T1[:, 0:TOK]), group(1), gate, ALU.mult).then_inc(taken[1], 1)
                            dve.wait_ge(taken[1], n0 // 2 + j + 1)
                            out = acc if mode == "middle" else tokens(T3[:, 0:TOK])
                            last = V_.tensor_tensor(out, acc, tokens(T1[:, 0:TOK]), ALU.add)
                            if mode == "last":
                                last.then_inc(sum_ready, 1)
                                dve.wait_ge(m_hi, j + 1)
                                V_.tensor_tensor(tile_at(M_LO, j), tokens(T3[:, 0:TOK]),
                                                 tile_at(M_HI, j).bitcast(F32),
                                                 ALU.subtract).then_inc(m_lo, 1)

            def attention_jobs(n0, side, r_v, *work):
                heads = (NJ + 1) * (side - 1)

                def low(n, out, high):
                    dve.wait_ge(q_hi, heads + n + 1)
                    V_.tensor_tensor(out, group(k), high.bitcast(F32), ALU.subtract).then_inc(taken[k], 1)

                for m in range(NJ + 2):
                    k = m % 2
                    following(n0, m // 2, k)
                    if m == 2:
                        dve.wait_ge(rows_out, (R_B_C if side == 1 else R_C_C) + 1)
                        V_.tensor_copy(KS[:, PAST:PAST + DEC], K_T[:, SEQ:TOK]).then_inc(staged, 1)
                    if m == 4:
                        for y, (a, b) in enumerate(TRIPLES[:2]):
                            dve.wait_ge(v_hi, 2 * (side - 1) + y + 1)
                            src = PS[:, 6 + (r_v + y) % 2, 0:(b - a) * P].rearrange("p (t d) -> p t d", d=P)
                            V_.tensor_tensor(V_LO[:, a:b, :], src, V_HI[:, a:b, :].bitcast(F32),
                                             ALU.subtract).then_inc(v_lo, 1)
                    if m <= NJ:
                        select(*(work[m] if isinstance(work[0][0], tuple) and len(work) > 1 else work[0]))
                    elif side == 2:
                        for i in SEL[0:3]:
                            to_mask(i)
                    if m == 0:
                        low(0, tokens(K_LO[:, :]), tokens(K_HI[:, :]))
                    elif m > 1:
                        low(m - 1, tokens(Q_LO[:, m - 2, :]), tokens(Q_HI[:, m - 2, :]))
                for k in range(2):
                    dve.wait_ge(taken[k], n0 // 2 + 3)
                V_.tensor_tensor(QS[:, :].rearrange("p (j t) -> p j t", t=DEC),
                                 Q_HI[:, :, SEQ:TOK].bitcast(F32), Q_LO[:, :, SEQ:TOK].bitcast(F32),
                                 ALU.add).then_inc(staged, 1)

            def mask_max(pair, h):
                x, ub, n, window = pair["x"], pair["ub"], pair["n"], pair["window"]
                dve.wait_ge(s_done, 2 * x + h + 1)
                if h == 0 and pair["free"]:
                    dve.wait_ge(pt_done, pair["free"])
                if h == 0 and not window and not pair["sample"] and pair["x"] == SPARSE[1]["x"]:
                    dve.wait_ge(stored[2], 16 * 4)
                top, neg = stat[:, ub, 0, h:h + 1], stat[:, ub, 1, h:h + 1]
                out = probs_of(pair, h)
                if pair["mask"] is None:
                    V_.tensor_scalar(out, scores_of(pair, h), SCALE, None, ALU.mult, ALU.max,
                                     accum_out=top).then_inc(masked, 1)
                else:
                    V_.tensor_tensor_reduce(out=out, in0=scores_of(pair, h), in1=pair["mask"], scale=SCALE,
                                            scalar=-3.4e38, op0=ALU.add, op1=ALU.max,
                                            accum_out=top).then_inc(masked, 1)
                if not window:
                    dve.wait_ge(masked, 2 * x + h + 1)
                    V_.tensor_scalar(neg, top, -1.0, None, ALU.mult).then_inc(negated, 1)

            def invert(pair, h):
                x, ub = pair["x"], pair["ub"]
                dve.wait_ge(exp_done, 2 * x + h + 1)
                inv, p = stat[:, ub, 5, h:h + 1], probs_of(pair, h)
                V_.reciprocal(inv, stat[:, ub, 2, h:h + 1]).then_inc(inverse, 1)
                if h == 0:
                    dve.wait_ge(inverse, 2 * x + 1)
                    V_.tensor_scalar(p, p, inv, None, ALU.mult).then_inc(probs[0], 1)

            def window_step(ahead, after, pair):
                if after:
                    dve.wait_ge(sink_exp, after["x"] + 1)
                    den, inv = stat[:, after["ub"], 2, :], stat[:, after["ub"], 5, :]
                    step.mark(V_.tensor_tensor(den, den, stat[:, after["ub"], 4, :], ALU.add))
                if ahead:
                    mask_max(ahead, 0)
                if after:
                    step.wait()
                    V_.reciprocal(inv, den).then_inc(inverse, 2)
                if ahead:
                    mask_max(ahead, 1)
                if after:
                    dve.wait_ge(inverse, 2 * after["x"] + 2)
                    p = probs_of(after, 0)
                    V_.tensor_scalar(p, p, inv[:, 0:1], None, ALU.mult).then_inc(probs[0], 1)
                if ahead:
                    x, ub = ahead["x"], ahead["ub"]
                    dve.wait_ge(masked, 2 * x + 2)
                    V_.scalar_tensor_tensor(stat[:, ub, 1, :], stat[:, ub, 0, :], -1.0, ahead["negative"],
                                            ALU.mult, ALU.min).then_inc(negated, 2)
                if pair:
                    pt_low(pair, 0)
                    if pair["sample"]:
                        pt_low(pair, 1)
                if ahead:
                    dve.wait_ge(negated, 2 * x + 2)
                    V_.tensor_tensor(stat[:, ub, 3, :], stat[:, ub, 1, :], ahead["sinks"],
                                     ALU.add).then_inc(sink_shift, 1)

            def pt_low(pair, c):
                q = pair["q"] + c
                if pair["sample"]:
                    rows = DEC if c == 1 else P
                    dve.wait_ge(pt_hi, q + 1)
                    V_.tensor_copy(PT_S[0:rows, q % 2, P:2 * P], PS[0:rows, 4 + q % 2, P:2 * P]).then_inc(pt_lo, 1)
                else:
                    n = 2 * P * len(pair["chunks"][c])
                    dve.wait_ge(pt_hi, q + 1)
                    V_.tensor_tensor(PT_LO[:, q % 2, 0:n], PS[:, 4 + q % 2, 0:n],
                                     PT_HI[:, q % 2, 0:n].bitcast(F32), ALU.subtract).then_inc(pt_lo, 1)

            def output(pair):
                dve.wait_ge(o_hi, pair["o"] + 1)
                for g in groups_of(pair):
                    src, high, out = attn_sums(pair, g)
                    last = V_.tensor_tensor(out, src, high.bitcast(F32), ALU.subtract)
                last.then_inc(o_lo, 1)

            def attend(ps):
                window = ps[0]["window"]
                for pair in ps[0:2]:
                    if window:
                        window_step(pair, None, None)
                    else:
                        mask_max(pair, 0)
                        mask_max(pair, 1)
                if window:
                    window_step(None, ps[0], None)
                else:
                    invert(ps[0], 0)
                    invert(ps[0], 1)
                for y, pair in enumerate(ps):
                    ahead, count = front(ps, y), len(pair["chunks"])
                    after = ps[y + 1] if y + 1 < len(ps) else None
                    if window:
                        window_step(ahead, after, pair)
                    else:
                        early = after and after["ahead"] == 2
                        if early:
                            invert(after, 0)
                            invert(after, 1)
                        if ahead:
                            mask_max(ahead, 0)
                            mask_max(ahead, 1)
                        for c in range(max(count, 4)):
                            if c < count:
                                pt_low(pair, c)
                            if c <= 1 and after and not early:
                                invert(after, c)
                    if y > 0 and ps[y - 1]["last"]:
                        output(ps[y - 1])
                output(ps[-1])

            to_mask(SEL[3])
            gates(J_GA, "first", ((SEL[5], 2), (SEL[1], 1)), ((SEL[5], 2), (SEL[1], 1)))
            to_mask(SEL[5])
            select((NT, TOPK_S // 8))
            to_mask(NT)
            attention_jobs(J_B, 1, R_B_V, ((SEL[2], 4), (SEL[0], 2)))
            attend(WINDOW)
            dve.wait_ge(stored[1], 16 * 6)
            gates(J_GB, "middle", ((SEL[4], 2),), ((SEL[4], 2), (SEL[1], 1)))
            to_mask(SEL[4])
            attention_jobs(J_C, 2, R_C_V, ((SEL[2], 2), (SEL[1], 1)), ((SEL[2], 3), (SEL[1], 2)), ((SEL[2], 3), (SEL[1], 1)),
                           ((SEL[2], 2), (SEL[1], 3), (SEL[0], 3)), ((SEL[2], 2), (SEL[1], 1), (SEL[0], 3)))
            attend(SPARSE)
            gates(J_GC, "last")

            V_.memset(T0[:, 0:TOK], 0.0).then_inc(ssq_sum, 1)
            V_.memset(U[:, 0:2], 0.0)
            following(J_WO, 0, 0)
            following(J_WO, 0, 1)
            dve.wait_ge(xr_out, NT + 1)

            def residual(i, k):
                    j = 2 * i + k
                    done(J_WO, i, k)
                    V_.tensor_tensor(tile_at(X2, j), group(k), tile_at(X2, j), ALU.add).then_inc(taken[k], 1)
                    dve.wait_ge(taken[k], J_WO // 2 + i + 1)
                    dve.wait_ge(g_hi, j + 1)
                    V_.scalar_tensor_tensor(tile_at(G_LO, j), tile_at(X2, j), vec_at(j, V_NORM),
                                            tile_at(G_HI, j).bitcast(F32), ALU.mult,
                                            ALU.subtract).then_inc(g_lo, 1)
                    dve.wait_ge(res_sq, j + 1)
                    dve.wait_ge(ssq_sum, j + 1)
                    V_.tensor_tensor(T0[:, 0:TOK], T0[:, 0:TOK], T1[:, 0:TOK], ALU.add).then_inc(ssq_sum, 1)

            residual(0, 0)
            residual(0, 1)
            with dve.Fori(1, KT // 2) as i:
                for k in range(2):
                    following(J_WO, i, k)
                    residual(i, k)

            def second_norm():
                dve.wait_ge(ss_done, 1)
                V_.tensor_scalar(ss[0:96, 1, 0:11], PS[0:96, 6, 0:11], 1.0 / D, EPS,
                                 ALU.mult, ALU.add).then_inc(ss_var, 1)
                dve.wait_ge(ss_var, 1)
                rsqrt(96, ss[0:96, 1, 0:11], ss[0:96, 2, 0:11], ss_pow, 1).then_inc(ss_rstd, 1)
                following(J_FFN[0], 0, 1)
                for m in range(3):
                    a, b = 480 * m, min(480 * (m + 1), TOK)
                    dve.wait_ge(rb_done, m + 1)
                    V_.tensor_copy(T3[:, a:b], PS[:, 7 - m % 2, 0:b - a]).then_inc(rb_ready, 1)
                dve.wait_ge(rb_ready, 3)

            def ffn(g, f, f0):
                following(J_FFN[g], f, 0)
                if g == 0 and isinstance(f, int):
                    second_norm()
                done(J_FFN[g], f, 0)
                conv_input(0, T3)
                dve.wait_ge(taken[0], J_FFN[g] // 2 + f + 1)
                states(f + f0, FT, S_CF, N_CF)
                convolve([vec_at(f, V_CF + w * FT + f0) for w in range(3)], T1).then_inc(conv_out, 1)
                if not isinstance(f, int):
                    following(J_FFN[g], f, 1)
                done(J_FFN[g], f, 1)
                dve.wait_ge(silu_scaled, f + (f0 + 1))
                V_.tensor_tensor(tokens(T0[:, 0:TOK]), group(1), tokens(T0[:, 0:TOK]),
                                 ALU.mult).then_inc(taken[1], 1)
                dve.wait_ge(f_hi, f + (f0 + 1))
                V_.tensor_tensor(tile_at(F_LO, f), tokens(T0[:, 0:TOK]), tile_at(F_HI, f).bitcast(F32),
                                 ALU.subtract).then_inc(f_lo, 1)

            def down(g, i, k, more=True):
                if more:
                    following(J_DOWN[g], i, k)
                done(J_DOWN[g], i, k)
                j = 2 * i + k
                V_.tensor_tensor(tile_at(X2, j), group(k), tile_at(X2, j), ALU.add).then_inc(taken[k], 1)
                if g == len(FFN_GROUPS) - 1:
                    dve.wait_ge(res_sq, j + (KT + 1))
                    dve.wait_ge(ssq_sum, j + (KT + 2))
                    V_.tensor_tensor(T0[:, 0:TOK], T0[:, 0:TOK], T1[:, 0:TOK], ALU.add).then_inc(ssq_sum, 1)

            f0 = 0
            for g, nf in enumerate(FFN_GROUPS):
                if g == 0:
                    ffn(0, 0, 0)
                with dve.Fori(1 if g == 0 else 0, nf) as f:
                    if g == 0:
                        with step.loop(f - 1, nf - 1, 3):
                            ffn(g, f, f0)
                    else:
                        with step.loop(f, nf, 3):
                            ffn(g, f, f0)
                last_group = g == len(FFN_GROUPS) - 1
                if last_group:
                    dve.wait_ge(f_lo, FT)
                    V_.memset(T0[:, 0:TOK], 0.0).then_inc(ssq_sum, 1)
                with dve.Fori(0, KT // 2 - 1 if last_group else KT // 2) as i:
                    for k in range(2):
                        down(g, i, k)
                if last_group:
                    down(g, KT // 2 - 1, 0)
                    down(g, KT // 2 - 1, 1, more=False)
                f0 += nf

            dve.wait_ge(y_sums, 1)
            V_.tensor_scalar(ss[:, 1, 0:NT], PS[:, 7, 0:NT], 1.0 / D, EPS, ALU.mult, ALU.add)
            V_.tensor_scalar(ss[0:DEC, 1, NT:NT + 1], PS[0:DEC, 7, NT:NT + 1], 1.0 / D, EPS,
                             ALU.mult, ALU.add).then_inc(y_var, 1)
            dve.wait_ge(y_var, 1)
            rsqrt(P, ss[:, 1, 0:NT + 1], ss[:, 2, 0:NT + 1], y_pow, 1).then_inc(y_rstd, 1)
            dve.wait_ge(y_rstd, 1)
            for i in range(1, NT + 1, 2):
                dve.wait_ge(y_t, i + 1)
                V_.tensor_scalar(Y[:, i, :], PS[:, 2 * (i % 3):2 * (i % 3) + 2, :].rearrange("p b n -> p (b n)"),
                                 ss[:, 2, i:i + 1], None, ALU.mult).then_inc(y_ready[1], 1)


_INS = ["x_prompt", "x_sample", "state_conv_a", "cache_swa_k", "cache_swa_v", "cache_dsa_k", "cache_dsa_v",
        "cache_idx_k", "state_ffn_conv", "norm_mix", "w_in", "conv_a", "w_a_out", "attn_sinks", "w_swa_o",
        "w_dsa_o", "w_out", "norm_ffn", "w_gate", "w_up", "conv_ffn", "w_down", "norm_final"]
_OUTS = [(1, SEQ, D), (1, DEC, D),
         (1, 1, 2, D_CONV), (1, 1, P, NKV, HD), (1, 1, P, NKV, HD), (1, 1, SEQ, NKV, HD), (1, 1, SEQ, NKV, HD),
         (1, 1, SEQ, HD), (1, 1, 2, D_FF),
         (1, 1, 2, D_CONV), (1, 1, P, NKV, HD), (1, 1, P, NKV, HD), (1, 1, DEC, NKV, HD), (1, 1, DEC, NKV, HD),
         (1, 1, DEC, HD), (1, 1, 2, D_FF)]


def kernel(**inputs):
    import numpy as _np
    import concourse.bacc as _bacc
    from concourse import mybir as _mybir
    from concourse.bass_utils import run_bass_kernel_spmd as _run

    nc = _bacc.Bacc("TRN2", target_bir_lowering=False, num_devices=1, dynamic_dma_scratch_size=4096)
    arrays, ins = {}, {}
    for name in _INS:
        a = _np.ascontiguousarray(inputs[name])
        arrays[f"in_{name}"] = a
        ins[name] = nc.dram_tensor(f"in_{name}", a.shape, _mybir.dt.from_np(a.dtype), kind="ExternalInput").ap()
    outs = [nc.dram_tensor(f"out_{i}", shape, _mybir.dt.float32, kind="ExternalOutput").ap()
            for i, shape in enumerate(_OUTS)]
    build(nc, ins, outs)
    r = _run(nc, [arrays], core_ids=[0])
    return tuple(r.results[0][f"out_{i}"] for i in range(len(_OUTS)))
```
